# Optimizing a Trainium2 kernel written in Bass

```python
import jax
import jax.numpy as jnp
from jax import lax
import numpy as np

D_MODEL = 1024
BATCH = 1
SEQ = 1024
DEPTH = 1

HEAD_DIM = 64
ATTN_GROUPS = ((128, 1), (512, 4), (2048, 16))
HEADS_PER_GROUP = 4
N_ATTN_HEADS = HEADS_PER_GROUP * len(ATTN_GROUPS)
ATTN_WIDTH = N_ATTN_HEADS * HEAD_DIM
ATTN_OUT_WIDTH = HEADS_PER_GROUP * HEAD_DIM
LRU_WIDTH = D_MODEL
LRU_BLOCKS = 16
LRU_BLOCK_WIDTH = LRU_WIDTH // LRU_BLOCKS
LRU_C = 8.0
CONV_WIDTH = 4
N_EXPERTS = 16
CAPACITY_FACTOR = 2
EXPERT_FF = 2 * D_MODEL
ROPE_THETA = 10000.0
NORM_EPS = 1e-6
NEG_INF = -1e30
IN_WIDTH = 3 * ATTN_WIDTH + 2 * LRU_WIDTH + 2 * D_MODEL
IN_SPLITS = (ATTN_WIDTH, 2 * ATTN_WIDTH, 3 * ATTN_WIDTH, 3 * ATTN_WIDTH + LRU_WIDTH,
             3 * ATTN_WIDTH + 2 * LRU_WIDTH, 3 * ATTN_WIDTH + 2 * LRU_WIDTH + D_MODEL)

kernel_name = 'hybrid_dilated_attn_rglru_ec_moe_block'

def rms_norm(t, w):
    t32 = t.astype(jnp.float32)
    y = t32 * lax.rsqrt(jnp.mean(t32 * t32, axis=-1, keepdims=True) + NORM_EPS)
    return (y * w.astype(jnp.float32)).astype(t.dtype)

def modulate(t, shift, scale):
    return t * (1.0 + scale[:, None, :]) + shift[:, None, :]

def apply_rope(t, positions):
    half = HEAD_DIM // 2
    inv_freq = ROPE_THETA ** (-jnp.arange(half, dtype=jnp.float32) / half)
    ang = positions.astype(jnp.float32)[:, :, None, None] * inv_freq
    cos, sin = jnp.cos(ang), jnp.sin(ang)
    t32 = t.astype(jnp.float32)
    t1, t2 = t32[..., :half], t32[..., half:]
    return jnp.concatenate([t1 * cos - t2 * sin, t2 * cos + t1 * sin], axis=-1).astype(t.dtype)

def banded_attention(q, k, v, half):
    n, length, heads, dh = q.shape
    blk = half
    nb = -(-length // blk)
    extra = nb * blk - length
    q_b = jnp.pad(q, ((0, 0), (0, extra), (0, 0), (0, 0))).reshape(n, nb, blk, heads, dh)
    kv_pad = ((0, 0), (blk, blk + extra), (0, 0), (0, 0))
    k_b = jnp.pad(k, kv_pad).reshape(n, nb + 2, blk, heads, dh)
    v_b = jnp.pad(v, kv_pad).reshape(n, nb + 2, blk, heads, dh)

    def band(t):
        return jnp.concatenate([t[:, :-2], t[:, 1:-1], t[:, 2:]], axis=2)

    k_w, v_w = band(k_b), band(v_b)
    valid = jnp.pad(jnp.ones((length,), dtype=bool), (blk, blk + extra)).reshape(nb + 2, blk)
    valid_w = jnp.concatenate([valid[:-2], valid[1:-1], valid[2:]], axis=1)
    rel = jnp.arange(3 * blk)[None, :] - blk - jnp.arange(blk)[:, None]
    mask = (jnp.abs(rel) <= half)[None] & valid_w[:, None, :]
    s = jnp.einsum('nbqhd,nbkhd->nbhqk', q_b, k_w).astype(jnp.float32) * (dh ** -0.5)
    s = jnp.where(mask[None, :, None], s, NEG_INF)
    m = jnp.max(s, axis=-1, keepdims=True)
    p = jnp.exp(s - m)
    den = jnp.sum(p, axis=-1)
    o = jnp.einsum('nbhqk,nbkhd->nbqhd', p, v_w.astype(jnp.float32))
    o = o / jnp.swapaxes(den, 2, 3)[..., None]
    lse = jnp.swapaxes(m[..., 0] + jnp.log(den), 2, 3)
    o = o.reshape(n, nb * blk, heads, dh)[:, :length]
    lse = lse.reshape(n, nb * blk, heads)[:, :length]
    return o, lse

def dilated_window_attention(q, k, v, window, dilation):
    b, s, heads, dh = q.shape
    length = s // dilation

    def to_classes(t):
        return t.reshape(b, length, dilation, heads, dh).transpose(0, 2, 1, 3, 4).reshape(b * dilation, length, heads, dh)

    o, lse = banded_attention(to_classes(q), to_classes(k), to_classes(v), window // (2 * dilation))
    o = o.reshape(b, dilation, length, heads, dh).transpose(0, 2, 1, 3, 4).reshape(b, s, heads, dh)
    lse = lse.reshape(b, dilation, length, heads).transpose(0, 2, 1, 3).reshape(b, s, heads)
    return o, lse

def block_diag_linear(t, w):
    b, s, ch = t.shape
    y = jnp.einsum('bsnk,nkj->bsnj', t.reshape(b, s, LRU_BLOCKS, LRU_BLOCK_WIDTH), w.astype(t.dtype))
    return y.reshape(b, s, ch)

def rglru_coeffs(xc, w_a, b_a, w_x, b_x, lam):
    r = jax.nn.sigmoid(block_diag_linear(xc, w_a) + b_a.astype(jnp.float32))
    i = jax.nn.sigmoid(block_diag_linear(xc, w_x) + b_x.astype(jnp.float32))
    log_a = -LRU_C * r * jax.nn.softplus(-lam.astype(jnp.float32))
    a = jnp.exp(log_a)
    u = jnp.sqrt(-jnp.expm1(2.0 * log_a)) * (i * xc)
    return a, u

def linear_combine(e1, e2):
    a1, u1 = e1
    a2, u2 = e2
    return a1 * a2, a2 * u1 + u2

def mixer(h, positions, w_in, q_norm_w, k_norm_w, conv_w, conv_b, lru_w_a, lru_b_a, lru_w_x, lru_b_x,
          lru_lambda, w_attn_branch, w_lru_branch, w_out):
    b, s, _ = h.shape
    proj = h @ w_in
    q, k, v, xr, yr, g_attn, g_lru = jnp.split(proj, IN_SPLITS, axis=-1)

    q = apply_rope(rms_norm(q.reshape(b, s, N_ATTN_HEADS, HEAD_DIM), q_norm_w), positions)
    k = apply_rope(rms_norm(k.reshape(b, s, N_ATTN_HEADS, HEAD_DIM), k_norm_w), positions)
    v = v.reshape(b, s, N_ATTN_HEADS, HEAD_DIM)
    outs, lses = [], []
    for g, (window, dilation) in enumerate(ATTN_GROUPS):
        hs = slice(g * HEADS_PER_GROUP, (g + 1) * HEADS_PER_GROUP)
        o, lse = dilated_window_attention(q[:, :, hs], k[:, :, hs], v[:, :, hs], window, dilation)
        outs.append(o)
        lses.append(lse)
    grp_w = jax.nn.softmax(jnp.stack(lses), axis=0)
    attn = jnp.sum(grp_w[..., None] * jnp.stack(outs), axis=0).reshape(b, s, ATTN_OUT_WIDTH).astype(h.dtype)

    pad_l = CONV_WIDTH // 2
    pad_r = CONV_WIDTH - 1 - pad_l
    xc = lax.conv_general_dilated(xr, conv_w.astype(xr.dtype), window_strides=(1,), padding=[(pad_l, pad_r)],
                                  dimension_numbers=('NWC', 'WIO', 'NWC'), feature_group_count=LRU_WIDTH)
    xc = (xc + conv_b).astype(jnp.float32)
    a_f, u_f = rglru_coeffs(xc, lru_w_a[0], lru_b_a[0], lru_w_x[0], lru_b_x[0], lru_lambda[0])
    a_b, u_b = rglru_coeffs(xc, lru_w_a[1], lru_b_a[1], lru_w_x[1], lru_b_x[1], lru_lambda[1])
    _, h_fwd = lax.associative_scan(linear_combine, (a_f, u_f), axis=1)
    _, h_bwd = lax.associative_scan(linear_combine, (a_b, u_b), reverse=True, axis=1)
    lru = ((h_fwd + h_bwd) * jax.nn.gelu(yr.astype(jnp.float32))).astype(h.dtype)

    merged = jax.nn.sigmoid(g_attn) * (attn @ w_attn_branch) + jax.nn.sigmoid(g_lru) * (lru @ w_lru_branch)
    return merged @ w_out

def expert_choice_ffn(h, w_router, w_gate, w_up, w_down):
    b, s, _ = h.shape
    capacity = max(1, CAPACITY_FACTOR * s // N_EXPERTS)
    logits = jnp.einsum('bsd,de->bse', h, w_router).astype(jnp.float32)
    affinity = jax.nn.softmax(logits, axis=-1)
    gates, idx = lax.top_k(jnp.swapaxes(affinity, 1, 2), capacity)
    idx_e = jnp.swapaxes(idx, 0, 1)
    gates_e = jnp.swapaxes(gates, 0, 1).astype(h.dtype)
    bidx = jnp.arange(b)[:, None]

    def run_expert(args):
        ix, gt, wg, wu, wd = args
        xe = h[bidx, ix]
        he = jax.nn.silu(xe @ wg) * (xe @ wu)
        return (he @ wd) * gt[..., None]

    ys = lax.map(run_expert, (idx_e, gates_e, w_gate, w_up, w_down))
    return jnp.zeros_like(h).at[jnp.arange(b)[None, :, None], idx_e].add(ys)

def setup_inputs(seed: int = 0) -> dict:
    key = jax.random.key(seed)
    ks = jax.random.split(key, 26)

    def nrm(k, shape, scale):
        return jax.random.normal(k, shape, jnp.float32) * scale

    L = DEPTH
    a0 = jax.random.uniform(ks[14], (L, 2, LRU_WIDTH), jnp.float32, 0.9, 0.999)
    s0 = a0 ** (1.0 / LRU_C)
    lru_lambda = jnp.log(s0) - jnp.log1p(-s0)
    positions = (jnp.arange(SEQ, dtype=jnp.int32)[None, :]
                 + jax.random.randint(ks[2], (BATCH, 1), 0, 1024, dtype=jnp.int32))
    return {
        'x': nrm(ks[0], (BATCH, SEQ, D_MODEL), 1.0),
        'c': nrm(ks[1], (BATCH, D_MODEL), 1.0),
        'positions': positions,
        'w_ada': nrm(ks[3], (L, D_MODEL, 6 * D_MODEL), D_MODEL ** -0.5),
        'b_ada': nrm(ks[4], (L, 6 * D_MODEL), 0.01),
        'norm1_w': 1.0 + nrm(ks[5], (L, D_MODEL), 0.01),
        'w_in': nrm(ks[6], (L, D_MODEL, IN_WIDTH), D_MODEL ** -0.5),
        'q_norm_w': 1.0 + nrm(ks[7], (L, N_ATTN_HEADS, HEAD_DIM), 0.01),
        'k_norm_w': 1.0 + nrm(ks[8], (L, N_ATTN_HEADS, HEAD_DIM), 0.01),
        'conv_w': nrm(ks[9], (L, CONV_WIDTH, 1, LRU_WIDTH), CONV_WIDTH ** -0.5),
        'conv_b': nrm(ks[10], (L, LRU_WIDTH), 0.01),
        'lru_w_a': nrm(ks[11], (L, 2, LRU_BLOCKS, LRU_BLOCK_WIDTH, LRU_BLOCK_WIDTH), LRU_BLOCK_WIDTH ** -0.5),
        'lru_b_a': nrm(ks[12], (L, 2, LRU_WIDTH), 0.01),
        'lru_w_x': nrm(ks[13], (L, 2, LRU_BLOCKS, LRU_BLOCK_WIDTH, LRU_BLOCK_WIDTH), LRU_BLOCK_WIDTH ** -0.5),
        'lru_b_x': nrm(ks[15], (L, 2, LRU_WIDTH), 0.01),
        'lru_lambda': lru_lambda,
        'w_attn_branch': nrm(ks[16], (L, ATTN_OUT_WIDTH, D_MODEL), ATTN_OUT_WIDTH ** -0.5),
        'w_lru_branch': nrm(ks[17], (L, LRU_WIDTH, D_MODEL), LRU_WIDTH ** -0.5),
        'w_out': nrm(ks[18], (L, D_MODEL, D_MODEL), D_MODEL ** -0.5),
        'norm2_w': 1.0 + nrm(ks[19], (L, D_MODEL), 0.01),
        'w_router': nrm(ks[20], (L, D_MODEL, N_EXPERTS), D_MODEL ** -0.5),
        'w_gate': nrm(ks[21], (L, N_EXPERTS, D_MODEL, EXPERT_FF), D_MODEL ** -0.5),
        'w_up': nrm(ks[22], (L, N_EXPERTS, D_MODEL, EXPERT_FF), D_MODEL ** -0.5),
        'w_down': nrm(ks[23], (L, N_EXPERTS, EXPERT_FF, D_MODEL), EXPERT_FF ** -0.5),
    }

def reference(x, c, positions, w_ada, b_ada, norm1_w, w_in, q_norm_w, k_norm_w, conv_w, conv_b,
              lru_w_a, lru_b_a, lru_w_x, lru_b_x, lru_lambda, w_attn_branch, w_lru_branch, w_out,
              norm2_w, w_router, w_gate, w_up, w_down):
    c_act = jax.nn.silu(c)
    for l in range(DEPTH):
        mod = c_act @ w_ada[l] + b_ada[l]
        shift1, scale1, gate1, shift2, scale2, gate2 = jnp.split(mod, 6, axis=-1)
        h = modulate(rms_norm(x, norm1_w[l]), shift1, scale1)
        mix = mixer(h, positions, w_in[l], q_norm_w[l], k_norm_w[l], conv_w[l], conv_b[l], lru_w_a[l],
                    lru_b_a[l], lru_w_x[l], lru_b_x[l], lru_lambda[l], w_attn_branch[l], w_lru_branch[l], w_out[l])
        x = x + gate1[:, None, :] * mix
        h2 = modulate(rms_norm(x, norm2_w[l]), shift2, scale2)
        ffn = expert_choice_ffn(h2, w_router[l], w_gate[l], w_up[l], w_down[l])
        x = x + gate2[:, None, :] * ffn
    return x


_drawn_inputs = setup_inputs


def setup_inputs(seed=0):
    import zlib

    import numpy as np

    out = dict(_drawn_inputs(seed))
    spreads = {}
    factors = {'norm1_w': 4.856,
     'q_norm_w': 8.0,
     'k_norm_w': 8.0,
     'conv_b': 3.257,
     'lru_b_a': 8.0,
     'lru_b_x': 8.0,
     'norm2_w': 7.418}
    for name, (base, spread) in spreads.items():
        noise = np.random.default_rng([zlib.crc32(name.encode()), seed]).standard_normal(out[name].shape)
        drawn = base * np.exp(spread * noise) if base else spread * noise
        out[name] = jnp.asarray(drawn.astype(out[name].dtype))
    for name, factor in factors.items():
        out[name] = (out[name] * factor).astype(out[name].dtype)
    return out
```

```python
from contextlib import ExitStack

import numpy as np

import concourse.bass as bass
from concourse import mybir

P = 128
F32 = mybir.dt.float32
F32R = mybir.dt.float32r
I32 = mybir.dt.int32
U32 = mybir.dt.uint32
ALU = mybir.AluOpType
ACT = mybir.ActivationFunctionType
AX = mybir.AxisListType

D = 1024
T = 1024
KC = D // P
TT = T // P
HALF = 512
HD = 64
GROUPS = 3
ROWS = 32
SLOTS = 4
AW = GROUPS * SLOTS * HD
QK_CHUNKS = AW // P
E = 16
FF = 2 * D
CAP = 2 * T // E
EPS = 1e-6
NEG = -1e30
UNIT = 256
RAW = 3
IN_Q, IN_K, IN_V = 0, AW, 2 * AW
IN_XR = 3 * AW
IN_YR = IN_XR + D
IN_GA = IN_YR + D
IN_GL = IN_GA + D
G0_KEYS, G12_KEYS = 640, 256
KEYS = G0_KEYS + 2 * G12_KEYS
M0_PAD = P + 3
CONV = 4

C_ID = 0
C_ONE = C_ID + P
C_SEL = C_ONE + 1
C_ROT = C_SEL + 2 * ROWS - 2
C_M0 = C_ROT + P
C_M1 = C_M0 + G0_KEYS + M0_PAD + 1
C_M2 = C_M1 + G12_KEYS + P
C_FREQ = C_M2 + G12_KEYS
C_EPS = C_FREQ + 1
C_PI2 = C_EPS + 1
C_END = C_PI2 + 1

A_C, A_N1, A_N2, A_QN, A_KN, A_BADA = 0, 8, 16, 24, 30, 36
A_END = A_BADA + 48
B_CW, B_CB, B_BA, B_BX, B_LAM = 0, 32, 40, 56, 72
B_END = 88


def constants():
    c = np.zeros((P, C_END), np.float32)
    p = np.arange(P)
    c[:, C_ID:C_ID + P] = np.eye(P)
    c[:, C_ONE] = 1.0
    c[:, C_SEL + ROWS - 2:C_SEL + ROWS] = (p[:, None] // HD == np.arange(2)[None, :]) / HD
    half = HD // 2
    for m in range(P):
        if m % HD < half:
            c[m + half, C_ROT + m] = -1.0
        else:
            c[m - half, C_ROT + m] = 1.0
    y = np.arange(G0_KEYS + M0_PAD + 1)
    c[:, C_M0:C_M1] = np.where(np.abs(y[None] - M0_PAD - 4 * p[:, None]) <= 64, 0.0, NEG)
    y = np.arange(G12_KEYS + P)
    c[:, C_M1:C_M2] = np.where(np.abs(y[None] - P - p[:, None]) <= 64, 0.0, NEG)
    y = np.arange(G12_KEYS)
    c[:, C_M2:C_FREQ] = np.where((y[None] - p[:, None]) % 4 == 0, 0.0, NEG)
    inv = np.float32(10000.0) ** (-np.arange(half, dtype=np.float32) / np.float32(half))
    c[:, C_FREQ] = inv[p % half]
    c[:, C_EPS] = EPS
    c[:, C_PI2] = np.pi / 2
    return c


def fetch_plan():
    plan = [("ada", u, "dve") for u in range(8)]
    ada = lambda u: ("ada", u, "dve")
    plan += [("qk", 0, "dve"), ada(8)]
    for n in range(1, 6):
        plan += [("qk", n, "dve"), ada(7 + 2 * n), ada(8 + 2 * n)]
    plan += [("v", 0, "dve"), ada(19), ada(20), ("v", 1, "dve"), ada(21), ("v", 2, "dve"), ada(22), ada(23)]
    plan += [("xy", n, "dve") for n in range(KC)]
    for n in range(4):
        plan += [("ga", n, "dve"), ("gl", n, "dve"), ("lru", n, "pe"), ("attn", n, "pe")]
    plan += [("out", n, "dve") for n in range(4)]
    return plan


class Build:

    def __init__(self, nc, ctx, dram):
        self.nc, self.ctx, self.dram = nc, ctx, dram
        self.plan = fetch_plan()
        self.order = {(k, n): u for u, (k, n, _) in enumerate(self.plan)}
        split_kinds = ("qk", "v", "xy", "ga", "gl", "out")
        self.items = {}
        counts = {"ada": 0, "split": 0, "pe": 0}
        self.freed_by = []
        for kind, n, reader in self.plan:
            group = "ada" if kind == "ada" else "split" if kind in split_kinds else "pe"
            if group == "split":
                self.items[(kind, n)] = 2 * counts["split"]
            counts[group] += 1
            self.freed_by.append((group, counts[group]))
        self.raw_in = [self.sem(f"raw_in{s}") for s in range(RAW)]
        self.ada_read = self.sem("ada_read")
        self.raw_pe = self.sem("raw_pe")
        self.hi_ready = self.sem("hi_ready")
        self.split_ready = self.sem("split_ready")
        self.pair_done = self.sem("pair_done")
        self.out_read = self.sem("out_read")
        self.issued = 0

    def rings(self, ctx):
        self.raw = self.sb("raw_ring", [P, RAW, KC * UNIT], ctx=ctx)
        self.hi = self.sb("hi_ring", [P, 2, D], F32R, ctx)
        self.lo = self.sb("lo_ring", [P, 2, D], F32R, ctx)

    def sb(self, name, shape, dt=F32, ctx=None):
        return (ctx or self.ctx).enter_context(self.nc.sbuf_tensor(name, shape, dt))

    def ps(self, name, shape, ctx):
        return ctx.enter_context(self.nc.psum_tensor(name, shape, F32))

    def sem(self, name):
        return self.ctx.enter_context(self.nc.semaphore(name))

    def source(self, kind, n):
        d = self.dram
        w_in = d["w_in"][0].rearrange("(c p) n -> p c n", p=P)
        rows = lambda w: w.rearrange("(c p) n -> p c n", p=P)
        cols = lambda w, start: w[:, :, start:start + UNIT]
        if kind == "ada":
            return cols(rows(d["w_ada"][0]), n * UNIT)
        if kind == "qk":
            return cols(w_in, (IN_Q if n < 3 else IN_K) + (n % 3) * UNIT)
        if kind == "xy":
            return [w_in[:, :, start + n * P:start + (n + 1) * P] for start in (IN_XR, IN_YR)]
        if kind in ("v", "ga", "gl"):
            start = {"v": IN_V, "ga": IN_GA, "gl": IN_GL}[kind]
            return cols(w_in, start + n * UNIT)
        if kind == "lru":
            return cols(rows(d["w_lru_branch"][0]), n * UNIT)
        if kind == "attn":
            return cols(rows(d["w_attn_branch"][0]), n * UNIT)
        return rows(d["w_out"][0])[:, 2 * n:2 * n + 2, :]

    def unit(self, kind, n):
        s = self.order[(kind, n)] % RAW
        if kind == "out":
            return self.raw[:, s, :].rearrange("p (c n) -> p c n", c=2)
        c = 2 if kind == "attn" else KC
        return self.raw[:, s, 0:c * UNIT].rearrange("p (c n) -> p c n", c=c)

    def fetch_until(self, sp, kind, n):
        last = min(self.order[(kind, n)] + RAW, len(self.plan) - 1)
        while self.issued <= last:
            u = self.issued
            k, m, _ = self.plan[u]
            if u >= RAW:
                group, count = self.freed_by[u - RAW]
                if group == "ada":
                    sp.wait_ge(self.ada_read, count)
                elif k == "out" and self.plan[u - RAW][0] == "out":
                    sp.wait_ge(self.out_read, 1)
                elif group == "split":
                    sp.wait_ge(self.split_ready, 2 * count)
                else:
                    sp.wait_ge(self.raw_pe, count)
            if k == "xy":
                for i, src in enumerate(self.source(k, m)):
                    sp.dma_start(self.item(k, m, i), src).then_inc(self.raw_in[u % RAW], 16)
            else:
                sp.dma_start(self.unit(k, m), self.source(k, m)).then_inc(self.raw_in[u % RAW], 16)
            self.issued += 1

    def arrived(self, eng, kind, n):
        u = self.order[(kind, n)]
        fetches = sum(2 if k == "xy" else 1 for k, _, _ in self.plan[u % RAW:u + 1:RAW])
        eng.wait_ge(self.raw_in[u % RAW], 16 * fetches)

    def item(self, kind, n, i):
        raw = self.unit(kind, n)
        if kind == "xy":
            s = self.order[(kind, n)] % RAW
            return self.raw[:, s, i * D:(i + 1) * D].rearrange("p (c n) -> p c n", c=KC)
        if kind == "v":
            return raw[:, 4 * i:4 * i + 4, :]
        if kind == "out":
            return raw[:, i, :]
        return raw[:, :, i * P:(i + 1) * P]

    def shaped(self, ring, kind, slot):
        if kind == "v":
            return ring[:, slot, :].rearrange("p (c n) -> p c n", c=4)
        if kind == "out":
            return ring[:, slot, :]
        return ring[:, slot, :].rearrange("p (c n) -> p c n", c=KC)

    def split_high(self, act, kind, n, i):
        k = self.items[(kind, n)] + i
        self.arrived(act, kind, n)
        if k >= 2:
            act.wait_ge(self.pair_done, k - 1)
        self.nc.scalar.activation(self.shaped(self.hi, kind, k % 2), self.item(kind, n, i),
                                  ACT.Copy).then_inc(self.hi_ready, 1)

    def split_low(self, dve, kind, n, i):
        k = self.items[(kind, n)] + i
        dve.wait_ge(self.hi_ready, k + 1)
        self.nc.vector.tensor_tensor(self.shaped(self.lo, kind, k % 2), self.item(kind, n, i),
                                     self.shaped(self.hi, kind, k % 2).bitcast(F32),
                                     ALU.subtract).then_inc(self.split_ready, 1)

    def project(self, out2, kind, n, i, moving_hi, moving_lo):
        k = self.items[(kind, n)] + i
        self.nc.tensor.wait_ge(self.split_ready, k + 1)
        whi, wlo = (self.shaped(r, kind, k % 2) for r in (self.hi, self.lo))
        for half in range(2):
            cols = slice(half * HALF, (half + 1) * HALF)
            for c in range(KC):
                for w, a in ((whi, moving_hi), (whi, moving_lo), (wlo, moving_hi)):
                    last = self.nc.tensor.matmul(out2[:, cols], w[:, c, :], a[:, c, cols],
                                                 start=(c == 0 and w is whi and a is moving_hi),
                                                 stop=(c == KC - 1 and w is wlo))
        last.then_inc(self.pair_done, 1)
        return last


class Chain:

    def __init__(self, eng, sem):
        self.eng, self.sem, self.n = eng, sem, 0

    def __call__(self, instruction):
        instruction.then_inc(self.sem, 1)
        self.n += 1
        self.eng.wait_ge(self.sem, self.n)


def ada_unit(b, dve, chain, u, acc, acc_free, cact):
    b.arrived(dve, "ada", u)
    if u >= 2:
        dve.wait_ge(acc_free, u - 1)
    w = b.unit("ada", u)
    a = acc[:, u % 2, :]
    chain(b.nc.vector.tensor_scalar(a, w[:, 0, :], cact[:, 0:1], None, ALU.mult))
    for c in range(1, KC):
        ins = b.nc.vector.scalar_tensor_tensor(out=a, in0=w[:, c, :], scalar=cact[:, c:c + 1], in1=a,
                                               op0=ALU.mult, op1=ALU.add)
        if c < KC - 1:
            chain(ins)
    ins.then_inc(b.ada_read, 1)


def ada_sum(b, pe, u, acc, acc_free, ps_mod, ones_col):
    pe.wait_ge(b.ada_read, u + 1)
    for i in range(2):
        last = b.nc.tensor.matmul(ps_mod[:, 2 * u + i:2 * u + i + 1], acc[:, u % 2, i * P:(i + 1) * P],
                                  ones_col, start=True, stop=True)
    last.then_inc(acc_free, 1)


def stage_norm(b, g):
    nc, d = b.nc, b.dram
    with ExitStack() as ctx:
        x_in = [b.sem(f"x_in{i}") for i in range(2)]
        rows_in, const_in = b.sem("rows_in"), b.sem("const_in")
        par_ps, par_ready, silu_ready = b.sem("par_ps"), b.sem("par_ready"), b.sem("silu_ready")
        squares, std_ready, xn_ready = b.sem("squares"), b.sem("std_ready"), b.sem("xn_ready")
        xt_ps, xt_read, h_hi, h_lo = b.sem("xt_ps"), b.sem("xt_read"), b.sem("h_hi"), b.sem("h_lo")
        link = b.sem("norm_link")
        rows_a = b.sb("rows_a", [A_END, P], ctx=ctx)
        rows_b = b.sb("rows_b", [B_END, P], ctx=ctx)
        x = b.sb("x_tok", [P, TT, D], ctx=ctx)
        scratch = b.sb("square_scratch", [P, D], ctx=ctx)
        ss = b.sb("sum_squares", [P, TT], ctx=ctx)
        std = b.sb("std", [P, TT], ctx=ctx)
        rstd = b.sb("rstd", [P, TT], ctx=ctx)
        h32 = b.sb("h32", [P, 2, HALF], ctx=ctx)
        ps_par = b.ps("ps_par", [P, HALF], ctx)
        ps_mod = b.ps("ps_mod0", [P, HALF], ctx)
        ps_x = b.ps("ps_x", [P, 4, HALF], ctx)
        const, par_a, par_b, mod, cact, acc = g.const, g.par_a, g.par_b, g.mod, g.cact, g.acc
        x_dram = d["x"][0].rearrange("(t p) n -> p t n", p=P)
        block = ctx.enter_context(nc.Block())

        @block.sync
        def _(sp):
            sp.dma_start(const[:, :], d["const"]).then_inc(const_in, 16)
            sp.dma_start(x[:, 0:4, :], x_dram[:, 0:4, :]).then_inc(x_in[0], 16)
            b.fetch_until(sp, "ada", 0)
            sp.dma_start(x[:, 4:8, :], x_dram[:, 4:8, :]).then_inc(x_in[1], 16)
            b.fetch_until(sp, "ada", 7)

        @block.scalar
        def _(act):
            rows = lambda ap: ap.rearrange("(r p) -> r p", p=P)
            parts = [(rows_a, A_C, d["c"][0]), (rows_a, A_N1, d["norm1_w"][0]), (rows_a, A_N2, d["norm2_w"][0]),
                     (rows_a, A_QN, d["q_norm_w"][0].rearrange("h n -> (h n)")),
                     (rows_a, A_KN, d["k_norm_w"][0].rearrange("h n -> (h n)")),
                     (rows_a, A_BADA, d["b_ada"][0]),
                     (rows_b, B_CW, d["conv_w"][0].rearrange("w o n -> (w o n)")), (rows_b, B_CB, d["conv_b"][0]),
                     (rows_b, B_BA, d["lru_b_a"][0].rearrange("w n -> (w n)")),
                     (rows_b, B_BX, d["lru_b_x"][0].rearrange("w n -> (w n)")),
                     (rows_b, B_LAM, d["lru_lambda"][0].rearrange("w n -> (w n)"))]
            for tile, at, ap in parts:
                n = ap.shape[0] // P
                act.dma_start(tile[at:at + n, :], rows(ap)).then_inc(rows_in, 16)
            act.wait_ge(par_ready, 2)
            nc.scalar.activation(cact[:, :], par_a[:, A_C:A_C + KC], ACT.Silu).then_inc(silu_ready, 1)
            for t in range(TT):
                if t % 4 == 0:
                    act.wait_ge(x_in[t // 4], 16)
                if t:
                    act.wait_ge(squares, t)
                nc.scalar.activation(scratch[:, :], x[:, t, :], ACT.Square,
                                     accum_out=ss[:, t:t + 1]).then_inc(squares, 1)
            act.wait_ge(squares, TT)
            nc.scalar.activation(std[:, :], ss[:, :], ACT.Sqrt, scale=1.0 / D,
                                 bias=const[:, C_EPS:C_EPS + 1]).then_inc(std_ready, 1)
            for j in range(2 * KC):
                c, half = j // 2, j % 2
                act.wait_ge(xt_read, j + 1)
                nc.scalar.activation(g.h_hi[:, c, half * HALF:(half + 1) * HALF], h32[:, j % 2, :],
                                     ACT.Copy).then_inc(h_hi, 1)

        def low(dve, j):
            c, cols = j // 2, slice(j % 2 * HALF, (j % 2 + 1) * HALF)
            dve.wait_ge(h_hi, j + 1)
            nc.vector.tensor_tensor(g.h_lo[:, c, cols], h32[:, j % 2, :], g.h_hi[:, c, cols].bitcast(F32),
                                    ALU.subtract).then_inc(h_lo, 1)

        @block.vector
        def _(dve):
            chain = Chain(dve, link)
            dve.wait_ge(par_ps, 1)
            nc.vector.tensor_copy(par_a[:, :], ps_par[:, 0:A_END]).then_inc(par_ready, 1)
            nc.vector.tensor_copy(par_b[:, :], ps_par[:, P:P + B_END]).then_inc(par_ready, 1)
            dve.wait_ge(silu_ready, 1)
            for u in range(4):
                ada_unit(b, dve, chain, u, acc, g.acc_free, cact)
            dve.wait_ge(std_ready, 1)
            chain(nc.vector.reciprocal(rstd[:, :], std[:, :]))
            for t in range(TT):
                nc.vector.tensor_scalar(x[:, t, :], x[:, t, :], rstd[:, t:t + 1], None,
                                        ALU.mult).then_inc(xn_ready, 1)
            for u in range(4, 8):
                ada_unit(b, dve, chain, u, acc, g.acc_free, cact)
            dve.wait_ge(g.acc_free, 8)
            chain(nc.vector.tensor_tensor(mod[:, 0:16], ps_mod[:, 0:16], par_a[:, A_BADA:A_BADA + 16], ALU.add))
            chain(nc.vector.scalar_tensor_tensor(out=mod[:, 8:16], in0=mod[:, 8:16], scalar=1.0,
                                                 in1=par_a[:, A_N1:A_N1 + 8], op0=ALU.add, op1=ALU.mult))
            for j in range(2 * KC):
                c, half = j // 2, j % 2
                dve.wait_ge(xt_ps, j + 1)
                if j >= 2:
                    dve.wait_ge(h_lo, j - 1)
                nc.vector.tensor_scalar(h32[:, j % 2, :], ps_x[:, j % 4, :], mod[:, 8 + c:9 + c],
                                        mod[:, c:c + 1], ALU.mult, ALU.add).then_inc(xt_read, 1)
                if j:
                    low(dve, j - 1)
            low(dve, 2 * KC - 1)

        @block.tensor
        def _(pe):
            pe.wait_ge(const_in, 16)
            pe.wait_ge(rows_in, 16 * 11)
            nc.tensor.transpose(ps_par[:, 0:A_END], rows_a[:, :], const[0:A_END, C_ID:C_ID + A_END])
            nc.tensor.transpose(ps_par[:, P:P + B_END], rows_b[:, :],
                                const[0:B_END, C_ID:C_ID + B_END]).then_inc(par_ps, 1)
            for u in range(8):
                ada_sum(b, pe, u, acc, g.acc_free, ps_mod, const[:, C_ONE:C_ONE + 1])
            for j in range(2 * KC):
                c, half = j // 2, j % 2
                if j >= 4:
                    pe.wait_ge(xt_read, j - 3)
                for i in range(4):
                    t = 4 * half + i
                    pe.wait_ge(xn_ready, TT)
                    last = nc.tensor.transpose(ps_x[:, j % 4, i * P:(i + 1) * P], x[:, t, c * P:(c + 1) * P],
                                               const[:, C_ID:C_ID + P])
                last.then_inc(xt_ps, 1)


def stage_qkv(b, g):
    nc, d = b.nc, b.dram
    n_qk = 2 * QK_CHUNKS
    n_heads = 2 * n_qk
    n_v = GROUPS * TT
    with ExitStack() as ctx:
        pos_in, folded, trig = b.sem("pos_in"), b.sem("folded"), b.sem("trig")
        sq_ready, sum_done, rot_ps = b.sem("sq_ready"), b.sem("head_sums"), b.sem("rot_ps")
        rot_read, rotated = b.sem("rot_read"), b.sem("qk_rotated")
        std_ready, inverted, rstd_hi, rstd_lo = b.sem("qk_std"), b.sem("qk_rstd"), b.sem("rstd_hi"), b.sem("rstd_lo")
        spread_ps, normalised = b.sem("spread_ps"), b.sem("qk_normalised")
        v_ps, v_read, link, mod_ready = b.sem("v_ps"), b.sem("v_read"), b.sem("qkv_link"), b.sem("mod_ready")
        rot = b.sb("rotated", [P, T], ctx=ctx)
        rstd = rot[0:ROWS, :]
        r_split = b.sb("rstd_split", [2 * ROWS, T], F32R, ctx)
        head_rows = b.sb("head_rows", [2 * ROWS, n_heads, HD], F32R, ctx)
        spare = g.v[:, :, :, :].rearrange("p g t n -> p (g t n)").rearrange("p (s n) -> p s n", n=T)
        cos, sin, square, turns, raw_qk = (spare[:, 0, :], spare[:, 1, :], spare[:, 2, :], spare[:, 3, :],
                                           spare[:, 4:6, :])
        angle = rot
        pos = g.attn_t[:, 0, :].bitcast(I32)
        ps_a = b.ps("ps_proj", [P, 4, HALF], ctx)
        ps_s = b.ps("ps_headsums", [P, 2, HALF], ctx)
        ps_r = b.ps("ps_rot", [P, HALF], ctx)
        ps_mod = b.ps("ps_mod1", [P, HALF], ctx)
        const, par_a, mod, cact, acc = g.const, g.par_a, g.mod, g.cact, g.acc
        proj_out = lambda j: ps_a[:, 2 * (j % 2):2 * (j % 2) + 2, :].rearrange("p a n -> p (a n)")
        spread = [ps_r[:, :], ps_s[:, 0, :], ps_s[:, 1, :]]
        lag = 6
        item = lambda j: b.items[("qk", j // 2)] + j % 2
        place = lambda j: (g.q if j < QK_CHUNKS else g.k)[:, j % QK_CHUNKS, :]
        halves = [slice(0, HALF), slice(HALF, T)]
        block = ctx.enter_context(nc.Block())

        @block.sync
        def _(sp):
            sp.dma_start(pos[:, :], d["positions"].to_broadcast([P, T])).then_inc(pos_in, 16)
            b.fetch_until(sp, "v", 2)
            b.fetch_until(sp, "ada", 23)

        @block.scalar
        def _(act):
            for i in range(2):
                b.split_high(act, "qk", 0, i)
            for at in (0, ROWS):
                nc.scalar.activation(head_rows[at:at + ROWS, :, :],
                                     const[at:at + ROWS, C_ID + at:C_ID + at + n_heads].unsqueeze(2).to_broadcast(
                                         [ROWS, n_heads, HD]), ACT.Copy).then_inc(rstd_hi, 1)
            act.wait_ge(folded, 1)
            nc.scalar.activation(sin[:, :], angle[:, :], ACT.Sin).then_inc(trig, 1)
            nc.scalar.activation(cos[:, :], angle[:, :], ACT.Abs).then_inc(trig, 1)
            act.wait_ge(trig, 2)
            nc.scalar.activation(cos[:, :], cos[:, :], ACT.Sin, scale=-1.0,
                                 bias=const[:, C_PI2:C_PI2 + 1]).then_inc(trig, 1)
            for j in range(n_qk):
                act.wait_ge(b.pair_done, item(j) + 1)
                if j >= 1:
                    act.wait_ge(sum_done, j)
                if j >= 2:
                    act.wait_ge(rotated, j - 1)
                w = (A_QN if j < QK_CHUNKS else A_KN) + j % QK_CHUNKS
                nc.scalar.activation(square[:, :], proj_out(j), ACT.Square).then_inc(sq_ready, 1)
                nc.scalar.activation(raw_qk[:, j % 2, :], proj_out(j), ACT.Identity,
                                     scale=par_a[:, w:w + 1]).then_inc(sq_ready, 1)
                if j + 2 < n_qk:
                    b.split_high(act, "qk", (j + 2) // 2, j % 2)
                else:
                    b.split_high(act, "v", 0, j % 2)
            act.wait_ge(rotated, n_qk)
            act.wait_ge(sum_done, n_qk)
            nc.scalar.activation(rstd[:, :], ps_s[0:ROWS, :, :].rearrange("p a n -> p (a n)"), ACT.Sqrt,
                                 bias=const[0:ROWS, C_EPS:C_EPS + 1]).then_inc(std_ready, 1)
            act.wait_ge(rotated, n_qk)
            for at in range(n_v):
                act.wait_ge(v_ps, at + 1)
                nc.scalar.activation(g.v[:, at // TT, at % TT, :], ps_a[:, at % 4, 0:UNIT], ACT.Copy).then_inc(v_read, 1)
                if at == lag - 4:
                    act.wait_ge(inverted, 1)
                    nc.scalar.activation(r_split[0:ROWS, :], rstd[:, :], ACT.Copy).then_inc(rstd_hi, 1)
                if at % TT == TT - 1 and at < n_v - 1:
                    for i in range(2):
                        b.split_high(act, "v", at // TT + 1, i)

        @block.vector
        def _(dve):
            chain = Chain(dve, link)
            for i in range(2):
                b.split_low(dve, "qk", 0, i)
            two_pi = 2 * np.pi
            c1 = 6.28125
            c2 = float(np.round((two_pi - c1) * 2 ** 21) / 2 ** 21)
            c3 = two_pi - c1 - c2
            magic = 1.5 * 2 ** 23
            dve.wait_ge(pos_in, 16)
            chain(nc.vector.tensor_copy(angle[:, :], pos[:, :]))
            chain(nc.vector.tensor_scalar(angle[:, :], angle[:, :], const[:, C_FREQ:C_FREQ + 1], None, ALU.mult))
            chain(nc.vector.tensor_scalar(turns[:, :], angle[:, :], 1 / two_pi, magic, ALU.mult, ALU.add))
            chain(nc.vector.tensor_scalar(turns[:, :], turns[:, :], magic, None, ALU.subtract))
            for part in (c1, c2, c3):
                chain(nc.vector.scalar_tensor_tensor(out=angle[:, :], in0=turns[:, :], scalar=-part,
                                                     in1=angle[:, :], op0=ALU.mult, op1=ALU.add))
            bound = float(np.nextafter(np.float32(np.pi), np.float32(0)))
            nc.vector.tensor_scalar(angle[:, :], angle[:, :], bound, -bound, ALU.min,
                                    ALU.max).then_inc(folded, 1)
            dve.wait_ge(trig, 3)

            def rotate(j):
                raw = raw_qk[:, j % 2, :]
                if j:
                    dve.wait_ge(rotated, j)
                for h in range(2):
                    dve.wait_ge(rot_ps, 2 * j + h + 1)
                    nc.vector.tensor_tensor(rot[:, halves[h]], ps_r[:, :], sin[:, halves[h]], ALU.mult).then_inc(rot_read, 1)
                chain(nc.vector.tensor_tensor(raw, raw, cos[:, :], ALU.mult))
                dve.wait_ge(rot_read, 2 * j + 2)
                nc.vector.tensor_tensor(place(j), rot[:, :], raw, ALU.add).then_inc(rotated, 1)

            for j in range(n_qk):
                if j >= 1:
                    rotate(j - 1)
                ada_unit(b, dve, chain, 8 + j, acc, g.acc_free, cact)
                if j + 2 < n_qk:
                    b.split_low(dve, "qk", (j + 2) // 2, j % 2)
                else:
                    b.split_low(dve, "v", 0, j % 2)
            rotate(n_qk - 1)
            dve.wait_ge(std_ready, 1)
            nc.vector.reciprocal(rstd[:, :], rstd[:, :]).then_inc(inverted, 1)
            dve.wait_ge(rstd_hi, 3)
            nc.vector.tensor_tensor(r_split[ROWS:2 * ROWS, :], rstd[:, :], r_split[0:ROWS, :].bitcast(F32), ALU.subtract).then_inc(rstd_lo, 1)
            dve.wait_ge(rotated, n_qk)
            for at in range(n_v + lag):
                m = at - lag
                if m >= 0:
                    j, h = divmod(m, 2)
                    dve.wait_ge(spread_ps, m + 1)
                    qk = place(j)[:, halves[h]]
                    nc.vector.tensor_tensor(qk, qk, spread[m % 3], ALU.mult).then_inc(normalised, 1)
                if at in (TT - 1, 2 * TT - 1):
                    n = at // TT
                    for i in range(2):
                        b.split_low(dve, "v", n + 1, i)
                    ada_unit(b, dve, chain, 20 + n, acc, g.acc_free, cact)
                elif at in (2 * TT + 2, 2 * TT + 4):
                    ada_unit(b, dve, chain, 22 + (at - 2 * TT - 2) // 2, acc, g.acc_free, cact)
            dve.wait_ge(g.acc_free, 24)
            chain(nc.vector.tensor_tensor(mod[:, 16:48], ps_mod[:, 16:48], par_a[:, A_BADA + 16:A_BADA + 48],
                                          ALU.add))
            nc.vector.scalar_tensor_tensor(out=mod[:, 32:40], in0=mod[:, 32:40], scalar=1.0,
                                           in1=par_a[:, A_N2:A_N2 + 8], op0=ALU.add,
                                           op1=ALU.mult).then_inc(mod_ready, 1)

        @block.tensor
        def _(pe):
            def rotation(j):
                swap = lambda h: nc.tensor.matmul(ps_r[:, :], const[:, C_ROT:C_ROT + P], raw_qk[:, j % 2, halves[h]],
                                                  start=True, stop=True).then_inc(rot_ps, 1)
                pe.wait_ge(sq_ready, 2 * (j + 1))
                if j:
                    pe.wait_ge(rot_read, 2 * j)
                swap(0)
                at = C_SEL + ROWS - 2 - 2 * j
                for h in range(2):
                    last = nc.tensor.matmul(ps_s[0:ROWS, h, :], const[:, at:at + ROWS], square[:, halves[h]],
                                            start=(j == 0), stop=(j == n_qk - 1))
                last.then_inc(sum_done, 1)
                pe.wait_ge(rot_read, 2 * j + 1)
                swap(1)

            b.project(proj_out(0), "qk", 0, 0, g.h_hi, g.h_lo)
            for j in range(n_qk):
                if j + 1 < n_qk:
                    if j:
                        pe.wait_ge(sq_ready, 2 * j)
                    b.project(proj_out(j + 1), "qk", (j + 1) // 2, (j + 1) % 2, g.h_hi, g.h_lo)
                rotation(j)
                ada_sum(b, pe, 8 + j, acc, g.acc_free, ps_mod, const[:, C_ONE:C_ONE + 1])

            def spread_one(m):
                j, h = divmod(m, 2)
                if m == 0:
                    pe.wait_ge(rstd_lo, 1)
                    pe.wait_ge(rot_read, 2 * n_qk)
                if m >= 3:
                    pe.wait_ge(normalised, m - 2)
                two = head_rows[:, 2 * j:2 * j + 2, :].rearrange("p h n -> p (h n)")
                nc.tensor.matmul(spread[m % 3], two, r_split[:, halves[h]], start=True, stop=True).then_inc(spread_ps, 1)

            for at in range(n_v):
                n, t = divmod(at, TT)
                k = b.items[("v", n)]
                pe.wait_ge(b.split_ready, k + 2)
                if at >= 4:
                    pe.wait_ge(v_read, at - 3)
                for c in range(KC):
                    def tok(h):
                        if n == 0:
                            return h[:, c, t * P:(t + 1) * P]
                        by_class = h[:, c, :].rearrange("p (j r) -> p r j", r=4)
                        return by_class[:, t // 2, (t % 2) * P:(t % 2 + 1) * P]
                    w = lambda ring: b.shaped(ring, "v", (k + c // 4) % 2)[:, c % 4, :]
                    for m, (a, r) in enumerate(((g.h_hi, b.hi), (g.h_lo, b.hi), (g.h_hi, b.lo))):
                        last = nc.tensor.matmul(ps_a[:, at % 4, 0:UNIT], tok(a), w(r),
                                                start=(c == 0 and m == 0), stop=(c == KC - 1 and m == 2))
                last.then_inc(v_ps, 1)
                if t == TT - 1:
                    pe.wait_ge(v_ps, at + 1)
                    pe.sem_inc(b.pair_done, 2)
                if at >= lag:
                    spread_one(at - lag)
                if at in (TT + 2, 2 * TT + 2):
                    ada_sum(b, pe, 20 + at // TT - 1, acc, g.acc_free, ps_mod, const[:, C_ONE:C_ONE + 1])
            for m in range(n_v - lag, n_v):
                spread_one(m)
            for u in (22, 23):
                ada_sum(b, pe, u, acc, g.acc_free, ps_mod, const[:, C_ONE:C_ONE + 1])


def stage_attention(b, g):
    nc = b.nc
    units = [(c, i, s) for c in range(4) for i in range(2) for s in range(SLOTS)]
    n_units = len(units)
    with ExitStack() as ctx:
        s_ps, s_read, max_ready, p_ready = b.sem("s_ps"), b.sem("s_read"), b.sem("max_ready"), b.sem("p_ready")
        t_ps, t_read_act, t_read_dve = b.sem("t_ps"), b.sem("t_read_act"), b.sem("t_read_dve")
        pv_done, o_read, link = b.sem("pv_done"), b.sem("o_read"), b.sem("attn_link")
        prob = b.sb("prob", [P, 2, KEYS], ctx=ctx)
        prob_t = b.sb("prob_t", [P, KEYS], ctx=ctx)
        stat = b.sb("stat", [P, 4, 6], ctx=ctx)
        attn = g.acc
        ps_s = b.ps("ps_s", [P, 3, HALF], ctx)
        ps_t = b.ps("ps_t", [P, 3, HALF], ctx)
        ps_o = b.ps("ps_o", [P, 2, HALF], ctx)
        const = g.const
        flat_s = ps_s[:, :, :].rearrange("p a n -> p (a n)")
        flat_t = ps_t[:, :, :].rearrange("p a n -> p (a n)")
        ident = const[:, C_ID:C_ID + P]
        block = ctx.enter_context(nc.Block())

        def classes(ap):
            return ap.rearrange("p (j r) -> p r j", r=4)

        def heads(t, group, s):
            base = HD * (s % 2)
            return t[base:base + HD, 2 * group + s // 2, :]

        @block.tensor
        def _(pe):
            def scores(u):
                c, i, s = units[u]
                if u:
                    pe.wait_ge(s_read, u)
                for group in range(GROUPS):
                    q = classes(heads(g.q, group, s))[:, c, i * P:(i + 1) * P]
                    k = heads(g.k, group, s)
                    if group == 0:
                        at = 384 * i
                        parts = [(0, k[:, at:at + HALF]), (HALF, k[:, at + HALF:at + G0_KEYS])]
                    else:
                        parts = [((G0_KEYS, 2 * HALF)[group - 1], classes(k)[:, c, :])]
                    for col, keys in parts:
                        last = nc.tensor.matmul(flat_s[:, col:col + keys.shape[1]], q, keys, start=True, stop=True)
                last.then_inc(s_ps, 1)

            def transpose(u):
                pe.wait_ge(p_ready, u + 1)
                if u:
                    pe.wait_ge(t_read_act, u)
                    pe.wait_ge(t_read_dve, u)
                if u >= 5 and u % 4 == 1:
                    attn_out(u // 4 - 1)
                for n in range(KEYS // P):
                    last = nc.tensor.transpose(flat_t[:, n * P:(n + 1) * P], prob[:, u % 2, n * P:(n + 1) * P], ident)
                last.then_inc(t_ps, 1)

            def attn_out(tile):
                pe.wait_ge(o_read, SLOTS * (tile + 1))
                for ch in range(2):
                    last = nc.tensor.transpose(ps_t[:, 2, (1 + ch) * P:(2 + ch) * P],
                                               attn[:, tile % 2, ch * P:(ch + 1) * P], ident)
                return last

            def values(u):
                c, i, s = units[u]
                pe.wait_ge(t_read_act, u + 1)
                pe.wait_ge(t_read_dve, u + 1)
                if u >= 2:
                    pe.wait_ge(o_read, u - 1)
                tiles = [(0, 3 * i + n) for n in range(5)] + [(1, 2 * c), (1, 2 * c + 1), (2, 2 * c), (2, 2 * c + 1)]
                for n, (group, t) in enumerate(tiles):
                    last = nc.tensor.matmul(ps_o[:, u % 2, 0:HD], prob_t[:, n * P:(n + 1) * P],
                                            g.v[:, group, t, s * HD:(s + 1) * HD],
                                            start=(n == 0), stop=(n == len(tiles) - 1))
                last.then_inc(pv_done, 1)

            for step in range(n_units + 2):
                if step < n_units:
                    scores(step)
                if 1 <= step <= n_units:
                    transpose(step - 1)
                if step >= 2:
                    values(step - 2)
            pe.wait_ge(t_read_dve, n_units)
            attn_out(7).then_inc(t_ps, 1)

        @block.scalar
        def _(act):
            def evacuate(u):
                act.wait_ge(t_ps, u + 1)
                if u:
                    act.wait_ge(pv_done, u)
                nc.scalar.activation(prob_t[:, 0:HALF], ps_t[:, 0, :], ACT.Copy).then_inc(t_read_act, 1)

            for i in range(2):
                b.split_high(act, "xy", 0, i)
            for u in range(n_units):
                act.wait_ge(max_ready, u + 1)
                nc.scalar.activation(prob[:, u % 2, :], prob[:, u % 2, :], ACT.Exp, bias=stat[:, u % 4, 3:4],
                                     accum_out=stat[:, u % 4, 4:5]).then_inc(p_ready, 1)
                if u:
                    evacuate(u - 1)
            evacuate(n_units - 1)

        @block.vector
        def _(dve):
            chain = Chain(dve, link)

            def maximum(u):
                c, i, s = units[u]
                st = stat[:, u % 4, :]
                if u >= 2:
                    dve.wait_ge(t_ps, u - 1)
                dve.wait_ge(s_ps, u + 1)
                m0, m1 = C_M0 + M0_PAD - c - P * i, C_M1 + P - P * i
                parts = [(0, 0, G0_KEYS, m0), (G0_KEYS, G0_KEYS, G12_KEYS, m1),
                         (G0_KEYS + G12_KEYS, 2 * HALF, G12_KEYS, C_M2)]
                for n, (dst, src, width, mask) in enumerate(parts):
                    ins = nc.vector.tensor_tensor_reduce(
                        out=prob[:, u % 2, dst:dst + width], in0=flat_s[:, src:src + width],
                        in1=const[:, mask:mask + width], scale=HD ** -0.5,
                        scalar=st[:, n - 1:n] if n else -3e38, op0=ALU.add, op1=ALU.max,
                        accum_out=st[:, n:n + 1])
                    if n < 2:
                        chain(ins)
                ins.then_inc(s_read, 1)
                dve.wait_ge(s_read, u + 1)
                nc.vector.tensor_scalar(st[:, 3:4], st[:, 2:3], -1.0, None, ALU.mult).then_inc(max_ready, 1)

            def attn_evacuate(tile):
                c, i = divmod(tile, 2)
                out = g.attn_t[:, :, :].rearrange("p a (j r) -> p a r j", r=4)[:, :, c, i * P:(i + 1) * P]
                return nc.vector.tensor_copy(out, ps_t[:, 2, P:3 * P].rearrange("p (a n) -> p a n", a=2))

            def evacuate(u):
                dve.wait_ge(t_ps, u + 1)
                if u:
                    dve.wait_ge(pv_done, u)
                if u >= 5 and u % 4 == 1:
                    attn_evacuate(u // 4 - 1)
                nc.vector.tensor_copy(prob_t[:, HALF:KEYS], flat_t[:, HALF:KEYS]).then_inc(t_read_dve, 1)

            def normalise(u):
                tile, s = divmod(u, SLOTS)
                st = stat[:, u % 4, :]
                dve.wait_ge(pv_done, u + 1)
                chain(nc.vector.reciprocal(st[:, 5:6], st[:, 4:5]))
                nc.vector.tensor_scalar(attn[:, tile % 2, s * HD:(s + 1) * HD], ps_o[:, u % 2, 0:HD],
                                        st[:, 5:6], None, ALU.mult).then_inc(o_read, 1)

            for i in range(2):
                b.split_low(dve, "xy", 0, i)
            for step in range(n_units + 2):
                if step < n_units:
                    maximum(step)
                if 1 <= step <= n_units:
                    evacuate(step - 1)
                if step >= 2:
                    normalise(step - 2)
            dve.wait_ge(t_ps, n_units + 1)
            attn_evacuate(7).then_inc(t_read_dve, 1)


def stage_lru(b, g):
    nc, d = b.nc, b.dram
    with ExitStack() as ctx:
        names = ["gate_in", "wg_hi", "wg_lo", "zeroed", "conv_done", "xc_hi", "xc_lo", "gates_f", "gates_b",
                 "tanh_f", "tanh_b", "a2_f", "a2_b", "z_f", "z_b", "ix_f", "ix_b", "sqrt_f", "sqrt_b", "u_f", "u_b",
                 "scan_f", "lru_done", "gelu_done", "lam_exp", "decay"]
        sem = {n: b.sem("lru_" + n) for n in names}
        link_dve, link_act = b.sem("lru_link_dve"), b.sem("lru_link_act")
        wg = g.acc[:, :, :].rearrange("p a (w n) -> p (a w) n", n=P)
        wg_hi, wg_lo = b.sb("wg_hi", [P, 4, P], F32R, ctx), b.sb("wg_lo", [P, 4, P], F32R, ctx)
        xc = b.sb("xc", [P, 2, T], ctx=ctx)
        xc_hi, xc_lo = b.sb("xc_hi", [P, T], F32R, ctx), b.sb("xc_lo", [P, T], F32R, ctx)
        recur, inp = b.sb("tanh_r", [P, 2, T], ctx=ctx), b.sb("tanh_i", [P, 2, T], ctx=ctx)
        decay, root = b.sb("decay", [P, 2, T], ctx=ctx), b.sb("root", [P, 2, T], ctx=ctx)
        small = b.sb("small", [P, 4, 16], ctx=ctx)
        c4, c4n, half_bias = b.sb("c4", [P, 16], ctx=ctx), b.sb("c4n", [P, 16], ctx=ctx), b.sb("hb", [P, 32], ctx=ctx)
        ps_x, ps_y = b.ps("ps_xr", [P, 2, HALF], ctx), b.ps("ps_yr", [P, 2, HALF], ctx)
        ps_ga, ps_gx = b.ps("ps_gate_a", [P, 2, HALF], ctx), b.ps("ps_gate_x", [P, 2, HALF], ctx)
        flat = lambda t: t[:, :, :].rearrange("p a n -> p (a n)")
        par = g.par_b
        col = lambda at: par[:, at:at + 1]
        item = lambda j, i: b.items[("xy", j)] + i
        F, B = 0, 1
        block = ctx.enter_context(nc.Block())

        @block.sync
        def _(sp):
            b.fetch_until(sp, "xy", KC - 1)

        @block.gpsimd
        def _(pool):
            nc.gpsimd.memset(wg[:, :, :], 0.0).then_inc(sem["zeroed"], 1)
            pool.wait_ge(sem["zeroed"], 1)
            for j in range(KC):
                if j:
                    pool.wait_ge(sem["wg_lo"], j)
                for w, name in enumerate(("lru_w_a", "lru_w_x")):
                    for h in range(2):
                        dst = wg[HD * h:HD * (h + 1), w::2, HD * h:HD * (h + 1)]
                        src = d[name][0, :, 2 * j + h].rearrange("w k n -> k w n")
                        pool.dma_start(dst, src).then_inc(sem["gate_in"], 16)

        @block.scalar
        def _(act):
            link = Chain(act, link_act)

            def gate_weights(j):
                act.wait_ge(sem["gate_in"], 64 * (j + 1))
                if j:
                    act.wait_ge(sem["gates_b"], j)
                nc.scalar.activation(wg_hi[:, :, :], wg[:, :, :], ACT.Copy).then_inc(sem["wg_hi"], 1)

            def conv_high(j):
                act.wait_ge(sem["conv_done"], j + 1)
                if j:
                    act.wait_ge(sem["gates_b"], j)
                nc.scalar.activation(xc_hi[:, :], xc[:, j % 2, :], ACT.Copy).then_inc(sem["xc_hi"], 1)

            def gelu(j):
                act.wait_ge(b.pair_done, item(j, 1) + 1)
                nc.scalar.activation(g.lru_t[:, j, :], flat(ps_y), ACT.Gelu_apprx_tanh).then_inc(sem["gelu_done"], 1)

            def direction(j, way, gates, tanh, z_done, u_done, last_read, a2_done):
                k = KC * way + j
                act.wait_ge(sem[gates], j + 1)
                if j:
                    act.wait_ge(sem[z_done], j)
                nc.scalar.activation(recur[:, way, :], flat(ps_ga), ACT.Tanh, scale=0.5,
                                     bias=half_bias[:, k:k + 1]).then_inc(sem[tanh], 1)
                if j:
                    act.wait_ge(sem[last_read], j)
                nc.scalar.activation(inp[:, way, :], flat(ps_gx), ACT.Tanh, scale=0.5,
                                     bias=half_bias[:, 16 + k:17 + k]).then_inc(sem[tanh], 1)
                act.wait_ge(sem[tanh], 2 * j + 1)
                link(nc.scalar.activation(decay[:, way, :], recur[:, way, :], ACT.Exp, scale=c4[:, k:k + 1],
                                          bias=c4[:, k:k + 1]))
                link(nc.scalar.activation(root[:, way, :], recur[:, way, :], ACT.Tanh, scale=c4n[:, k:k + 1],
                                          bias=c4n[:, k:k + 1]))
                nc.scalar.activation(recur[:, way, :], decay[:, way, :], ACT.Square).then_inc(sem[a2_done], 1)

            link(nc.scalar.activation(small[:, 0, :], par[:, B_LAM:B_LAM + 16], ACT.Abs))
            nc.scalar.activation(small[:, 0, :], small[:, 0, :], ACT.Exp, scale=-1.0).then_inc(sem["lam_exp"], 1)
            gate_weights(0)
            for i in range(2):
                b.split_high(act, "xy", 1, i)
            conv_high(0)
            gelu(0)
            act.wait_ge(sem["decay"], 1)
            def next_item(j, i):
                if j + 2 < KC:
                    b.split_high(act, "xy", j + 2, i)
                elif j + 2 == KC:
                    b.split_high(act, "ga", 0, i)

            for j in range(KC):
                next_item(j, 0)
                direction(j, F, "gates_f", "tanh_f", "z_f", "u_f", "scan_f", "a2_f")
                next_item(j, 1)
                direction(j, B, "gates_b", "tanh_b", "z_b", "u_b", "lru_done", "a2_b")
                if j + 1 < KC:
                    gate_weights(j + 1)
                    conv_high(j + 1)
                for way, z, done in ((F, "z_f", "sqrt_f"), (B, "z_b", "sqrt_b")):
                    act.wait_ge(sem[z], j + 1)
                    nc.scalar.activation(root[:, way, :], root[:, way, :], ACT.Sqrt).then_inc(sem[done], 1)
                if j + 1 < KC:
                    gelu(j + 1)

        @block.vector
        def _(dve):
            link = Chain(dve, link_dve)

            def conv(j):
                dve.wait_ge(b.pair_done, item(j, 0) + 1)
                if j >= 2:
                    dve.wait_ge(sem["lru_done"], j - 1)
                y, x = xc[:, j % 2, :], flat(ps_x)
                w = lambda tap: col(B_CW + KC * tap + j)
                link(nc.vector.tensor_scalar(y, x, w(2), col(B_CB + j), ALU.mult, ALU.add))
                for tap, dst, src in ((0, y[:, 2:T], x[:, 0:T - 2]), (1, y[:, 1:T], x[:, 0:T - 1]),
                                      (3, y[:, 0:T - 1], x[:, 1:T])):
                    ins = nc.vector.scalar_tensor_tensor(out=dst, in0=src, scalar=w(tap), in1=dst,
                                                         op0=ALU.mult, op1=ALU.add)
                    if tap < 3:
                        link(ins)
                ins.then_inc(sem["conv_done"], 1)

            def lows(j):
                dve.wait_ge(sem["wg_hi"], j + 1)
                nc.vector.tensor_tensor(wg_lo[:, :, :], wg[:, :, :], wg_hi[:, :, :].bitcast(F32),
                                        ALU.subtract).then_inc(sem["wg_lo"], 1)
                dve.wait_ge(sem["xc_hi"], j + 1)
                nc.vector.tensor_tensor(xc_lo[:, :], xc[:, j % 2, :], xc_hi[:, :].bitcast(F32),
                                        ALU.subtract).then_inc(sem["xc_lo"], 1)

            def before_root(j, way, a2, z, tanh, ix):
                dve.wait_ge(sem[a2], j + 1)
                nc.vector.scalar_tensor_tensor(out=root[:, way, :], in0=recur[:, way, :], scalar=1.0,
                                               in1=root[:, way, :], op0=ALU.add, op1=ALU.mult).then_inc(sem[z], 1)
                dve.wait_ge(sem[tanh], 2 * j + 2)
                nc.vector.scalar_tensor_tensor(out=inp[:, way, :], in0=inp[:, way, :], scalar=1.0,
                                               in1=xc[:, j % 2, :], op0=ALU.add, op1=ALU.mult).then_inc(sem[ix], 1)

            def after_root(j, way, root_done, ix, u):
                dve.wait_ge(sem[root_done], j + 1)
                dve.wait_ge(sem[ix], j + 1)
                nc.vector.scalar_tensor_tensor(out=inp[:, way, :], in0=inp[:, way, :], scalar=0.5,
                                               in1=root[:, way, :], op0=ALU.mult, op1=ALU.mult).then_inc(sem[u], 1)
                dve.wait_ge(sem[u], j + 1)

            e, s, s2, q = (small[:, n, :] for n in range(4))
            dve.wait_ge(sem["lam_exp"], 1)
            link(nc.vector.tensor_scalar(s, e, 2.0, None, ALU.add))
            link(nc.vector.reciprocal(s, s))
            link(nc.vector.tensor_tensor(s, e, s, ALU.mult))
            link(nc.vector.tensor_tensor(s2, s, s, ALU.mult))
            link(nc.vector.tensor_scalar(q, s2, 1.0 / 17, None, ALU.mult))
            for n in (15, 13, 11, 9, 7, 5, 3):
                link(nc.vector.scalar_tensor_tensor(out=q, in0=q, scalar=1.0 / n, in1=s2, op0=ALU.add, op1=ALU.mult))
            link(nc.vector.scalar_tensor_tensor(out=q, in0=q, scalar=1.0, in1=s, op0=ALU.add, op1=ALU.mult))
            link(nc.vector.tensor_scalar(q, q, 2.0, None, ALU.mult))
            link(nc.vector.tensor_scalar(s, par[:, B_LAM:B_LAM + 16], -1.0, 0.0, ALU.mult, ALU.max))
            link(nc.vector.tensor_tensor(q, q, s, ALU.add))
            link(nc.vector.tensor_scalar(c4[:, :], q, -4.0, None, ALU.mult))
            link(nc.vector.tensor_scalar(c4n[:, :], q, 4.0, None, ALU.mult))
            nc.vector.tensor_scalar(half_bias[:, :], par[:, B_BA:B_BA + 32], 0.5, None,
                                    ALU.mult).then_inc(sem["decay"], 1)
            conv(0)
            for i in range(2):
                b.split_low(dve, "xy", 1, i)
            lows(0)
            def next_item(j, i):
                if j + 2 < KC:
                    b.split_low(dve, "xy", j + 2, i)
                elif j + 2 == KC:
                    b.split_low(dve, "ga", 0, i)

            for j in range(KC):
                if j + 1 < KC:
                    conv(j + 1)
                next_item(j, 0)
                before_root(j, F, "a2_f", "z_f", "tanh_f", "ix_f")
                next_item(j, 1)
                before_root(j, B, "a2_b", "z_b", "tanh_b", "ix_b")
                if j + 1 < KC:
                    lows(j + 1)
                after_root(j, F, "sqrt_f", "ix_f", "u_f")
                h = xc[:, j % 2, :]
                dve.wait_ge(sem["ix_b"], j + 1)
                nc.vector.tensor_tensor_scan(h, decay[:, F, :], inp[:, F, :], 0.0, ALU.mult,
                                             ALU.add).then_inc(sem["scan_f"], 1)
                after_root(j, B, "sqrt_b", "ix_b", "u_b")
                back = inp[:, B, ::-1]
                link(nc.vector.tensor_tensor_scan(back, decay[:, B, ::-1], back, 0.0, ALU.mult, ALU.add))
                dve.wait_ge(sem["scan_f"], j + 1)
                link(nc.vector.tensor_tensor(h, h, inp[:, B, :], ALU.add))
                dve.wait_ge(sem["gelu_done"], j + 1)
                nc.vector.tensor_tensor(g.lru_t[:, j, :], g.lru_t[:, j, :], h, ALU.mult).then_inc(sem["lru_done"], 1)

        @block.tensor
        def _(pe):
            def gates(j, way, done):
                for a, out in ((0, ps_ga), (1, ps_gx)):
                    w = 2 * way + a
                    for h in range(2):
                        cols = slice(h * HALF, (h + 1) * HALF)
                        for m, (l, r) in enumerate(((wg_hi, xc_hi), (wg_hi, xc_lo), (wg_lo, xc_hi))):
                            last = nc.tensor.matmul(out[:, h, :], l[:, w, :], r[:, cols], start=(m == 0), stop=(m == 2))
                last.then_inc(sem[done], 1)

            b.project(flat(ps_x), "xy", 0, 0, g.h_hi, g.h_lo)
            b.project(flat(ps_y), "xy", 0, 1, g.h_hi, g.h_lo)
            for j in range(KC):
                if j + 1 < KC:
                    pe.wait_ge(sem["conv_done"], j + 1)
                    b.project(flat(ps_x), "xy", j + 1, 0, g.h_hi, g.h_lo)
                pe.wait_ge(sem["wg_lo"], j + 1)
                pe.wait_ge(sem["xc_lo"], j + 1)
                if j:
                    pe.wait_ge(sem["tanh_b"], 2 * j)
                gates(j, F, "gates_f")
                if j + 1 < KC:
                    pe.wait_ge(sem["gelu_done"], j + 1)
                    b.project(flat(ps_y), "xy", j + 1, 1, g.h_hi, g.h_lo)
                pe.wait_ge(sem["tanh_f"], 2 * j + 2)
                gates(j, B, "gates_b")


def stage_merge(b, g):
    nc = b.nc
    with ExitStack() as ctx:
        gate_tanh, branch_ps, merged_done = b.sem("gate_tanh"), b.sem("branch_ps"), b.sem("merged_done")
        lru_ps, lru_read, attn_read = b.sem("lru_branch_ps"), b.sem("lru_branch_read"), b.sem("attn_branch_read")
        gate = b.sb("gate", [P, 4, T], ctx=ctx)
        ps_g = b.ps("ps_gates", [P, 4, HALF], ctx)
        ps_l, ps_a = b.ps("ps_lru", [P, 2, HALF], ctx), b.ps("ps_attn", [P, 2, HALF], ctx)
        flat = lambda t: t[:, :, :].rearrange("p a n -> p (a n)")
        gate_out = lambda n: ps_g[:, 2 * (n % 2):2 * (n % 2) + 2, :].rearrange("p a n -> p (a n)")
        pairs = KC // 2
        kinds = [("ga", 0), ("ga", 1), ("gl", 0), ("gl", 1)]
        item = lambda n, q: b.items[(kinds[q][0], n)] + kinds[q][1]
        block = ctx.enter_context(nc.Block())

        @block.sync
        def _(sp):
            b.fetch_until(sp, "attn", pairs - 1)

        @block.scalar
        def _(act):
            for n in range(pairs):
                for q in range(4):
                    act.wait_ge(b.pair_done, item(n, q) + 1)
                    if n:
                        act.wait_ge(merged_done, 2 * n - 1 + q % 2)
                    nc.scalar.activation(gate[:, q, :], gate_out(q), ACT.Tanh, scale=0.5).then_inc(gate_tanh, 1)
                    if q < 2:
                        b.split_high(act, "gl", n, q)
                    elif n + 1 < pairs:
                        b.split_high(act, "ga", n + 1, q - 2)

        @block.vector
        def _(dve):
            for n in range(pairs):
                for q in range(4):
                    if q < 2:
                        b.split_low(dve, "gl", n, q)
                    elif n + 1 < pairs:
                        b.split_low(dve, "ga", n + 1, q - 2)
                dve.wait_ge(gate_tanh, 4 * n + 4)
                for i in range(2):
                    for q, ps, done, read in ((2 + i, ps_l, lru_ps, lru_read), (i, ps_a, branch_ps, attn_read)):
                        dve.wait_ge(done, 2 * n + i + 1)
                        nc.vector.scalar_tensor_tensor(out=gate[:, q, :], in0=gate[:, q, :], scalar=1.0,
                                                       in1=flat(ps), op0=ALU.add, op1=ALU.mult).then_inc(read, 1)
                    dve.wait_ge(lru_read, 2 * n + i + 1)
                    dve.wait_ge(attn_read, 2 * n + i + 1)
                    nc.vector.tensor_tensor(g.merged[:, 2 * n + i, :], gate[:, i, :], gate[:, 2 + i, :],
                                            ALU.add).then_inc(merged_done, 1)

        @block.tensor
        def _(pe):
            for n in range(pairs):
                for q, (kind, i) in enumerate(kinds):
                    if 4 * n + q >= 2:
                        pe.wait_ge(gate_tanh, 4 * n + q - 1)
                    b.project(gate_out(q), kind, n, i, g.h_hi, g.h_lo)
                w_lru, w_attn = b.unit("lru", n), b.unit("attn", n)
                b.arrived(pe, "lru", n)
                for i in range(2):
                    cols = slice(i * P, (i + 1) * P)
                    if 2 * n + i:
                        pe.wait_ge(lru_read, 2 * n + i)
                    for h in range(2):
                        for c in range(KC):
                            last = nc.tensor.matmul(ps_l[:, h, :], w_lru[:, c, cols],
                                                    g.lru_t[:, c, h * HALF:(h + 1) * HALF],
                                                    start=(c == 0), stop=(c == KC - 1))
                    last.then_inc(lru_ps, 1)
                    if i == 0:
                        b.arrived(pe, "attn", n)
                    if 2 * n + i:
                        pe.wait_ge(attn_read, 2 * n + i)
                    for h in range(2):
                        for c in range(2):
                            last = nc.tensor.matmul(ps_a[:, h, :], w_attn[:, c, cols],
                                                    g.attn_t[:, c, h * HALF:(h + 1) * HALF],
                                                    start=(c == 0), stop=(c == 1))
                    last.then_inc(branch_ps, 1)
                pe.wait_ge(branch_ps, 2 * n + 2)
                pe.sem_inc(b.raw_pe, 2)


def stage_out(b, g, out, h2_dram):
    nc, d = b.nc, b.dram
    with ExitStack() as ctx:
        names = ["router_in", "x_in0", "x_in1", "rows_ps", "rows_ready", "w_hi", "m_hi", "m_lo", "mix_ps",
                 "x1_ready", "square", "std", "h2_ready", "tr_ps", "tr_read", "logit_ps", "logits", "shifted",
                 "exped", "affinity", "aff_ps", "aff_ready", "chosen", "choice_ps", "stored_x1_0", "stored_x1_1", "stored_h2_0", "stored_h2_1"]
        sem = {n: b.sem("out_" + n) for n in names}
        link = b.sem("out_link")
        w_hi, w_lo = g.h_hi, g.h_lo
        spare = g.lru_t
        rows = lambda r: spare[:, r, :] if r < 2 else g.attn_t[:, 0, :]
        h2_t = g.attn_t[:, 1, :].rearrange("p (c n) -> p c n", n=P)
        x, x1, h2 = spare[:, 2:4, :], spare[:, 4:6, :], spare[:, 6:8, :]
        m_hi, m_lo = b.sb("m_hi", [P, 2, KC, P], F32R, ctx), b.sb("m_lo", [P, 2, KC, P], F32R, ctx)
        router = b.sb("router", [P, KC, E], ctx=ctx)
        stat = b.sb("out_stat", [P, 2, 3], ctx=ctx)
        logits, soft = b.sb("logits", [P, 4, 2, E], ctx=ctx), b.sb("soft", [P, 3, TT], ctx=ctx)
        ps_mix = b.ps("ps_mix", [P, 4, HALF], ctx)
        ps_tr, ps_log, ps_choice = b.ps("ps_tr", [P, 2, HALF], ctx), b.ps("ps_log", [P, HALF], ctx), b.ps("ps_choice", [P, HALF], ctx)
        const, mod = g.const, g.mod
        logits_flat = logits[:, :, :, :].rearrange("p a b e -> p (a b e)")
        by_tile = logits[:, :, :, :].rearrange("p a b e -> p (a b) e")
        ident = const[:, C_ID:C_ID + P]
        flat_tr = ps_tr[:, :, :].rearrange("p a n -> p (a n)")
        mix = lambda t: ps_mix[:, 2 * (t % 2):2 * (t % 2) + 2, :].rearrange("p a n -> p (a n)")
        aff = h2_t[0:2 * E, 0:4, :].rearrange("p c n -> p (c n)")
        best_at = b.sb("best_at", [2 * E, CAP], U32, ctx)
        lists = b.sb("best_lists", [2 * E, 4, CAP], ctx=ctx)
        best, best_at_f, best_up, best_at_up = (lists[:, n, :] for n in range(4))
        pick = b.sb("pick", [P, 2, E], ctx=ctx)
        x_dram = d["x"][0]
        block = ctx.enter_context(nc.Block())
        row_cols = [16, 32, 24]

        @block.sync
        def _(sp):
            sp.dma_start(router[:, :, :], d["w_router"][0].rearrange("(c p) n -> p c n", p=P)
                         ).then_inc(sem["router_in"], 16)
            for t in range(2):
                sp.dma_start(x[:, t, :], x_dram[t * P:(t + 1) * P, :]).then_inc(sem[f"x_in{t}"], 16)
            b.fetch_until(sp, "out", 3)
            for t in range(TT):
                sp.wait_ge(sem["x1_ready"], t + 1)
                sp.dma_start(out[0, t * P:(t + 1) * P, :], x1[:, t % 2, :]).then_inc(sem[f"stored_x1_{t % 2}"], 16)
                if t + 2 < TT:
                    sp.dma_start(x[:, t % 2, :], x_dram[(t + 2) * P:(t + 3) * P, :]).then_inc(sem[f"x_in{t % 2}"], 16)
                sp.wait_ge(sem["h2_ready"], t + 1)
                sp.dma_start(h2_dram[t * P:(t + 1) * P, :], h2[:, t % 2, :]).then_inc(sem[f"stored_h2_{t % 2}"], 16)
            for t in range(2):
                sp.wait_ge(sem[f"stored_x1_{t}"], 8 * TT)
                sp.wait_ge(sem[f"stored_h2_{t}"], 8 * TT)

        @block.scalar
        def _(act):
            for r in range(3):
                act.wait_ge(sem["rows_ps"], r + 1)
                nc.scalar.activation(rows(r), mix(r), ACT.Copy, scale=0.5 if r == 0 else 1.0
                                     ).then_inc(sem["rows_ready"], 1)

            def m_high(t):
                if t >= 2:
                    act.wait_ge(sem["mix_ps"], t - 1)
                nc.scalar.activation(m_hi[:, t % 2, :, :], g.merged[:, :, t * P:(t + 1) * P],
                                     ACT.Copy).then_inc(sem["m_hi"], 1)

            m_high(0)
            for n in range(4):
                b.arrived(act, "out", n)
                nc.scalar.activation(w_hi[:, 2 * n:2 * n + 2, :], b.unit("out", n), ACT.Copy).then_inc(sem["w_hi"], 1)
            m_high(1)
            for t in range(TT):
                act.wait_ge(sem["x1_ready"], t + 1)
                if t >= 2:
                    act.wait_ge(sem[f"stored_h2_{t % 2}"], 16 * (t // 2))
                    act.wait_ge(sem["tr_ps"], t - 1)
                nc.scalar.activation(h2[:, t % 2, :], x1[:, t % 2, :], ACT.Square,
                                     accum_out=stat[:, t % 2, 0:1]).then_inc(sem["square"], 1)
                act.wait_ge(sem["square"], t + 1)
                nc.scalar.activation(stat[:, t % 2, 1:2], stat[:, t % 2, 0:1], ACT.Sqrt, scale=1.0 / D,
                                     bias=const[:, C_EPS:C_EPS + 1]).then_inc(sem["std"], 1)
                if t + 2 < TT:
                    m_high(t + 2)
                act.wait_ge(sem["tr_ps"], t + 1)
                if t:
                    act.wait_ge(sem["logit_ps"], t)
                nc.scalar.activation(h2_t[:, :, :].rearrange("p c n -> p (c n)"), flat_tr,
                                     ACT.Copy).then_inc(sem["tr_read"], 1)
            act.wait_ge(sem["shifted"], 1)
            nc.scalar.activation(logits_flat, logits_flat, ACT.Exp).then_inc(sem["exped"], 1)
            act.wait_ge(sem["aff_ps"], 1)
            act.wait_ge(sem["logit_ps"], TT)
            nc.scalar.activation(aff, flat_tr[0:2 * E, 0:HALF], ACT.Copy).then_inc(sem["aff_ready"], 1)

        @block.vector
        def _(dve):
            chain = Chain(dve, link)

            def m_low(t):
                dve.wait_ge(sem["m_hi"], t + 1)
                nc.vector.tensor_tensor(m_lo[:, t % 2, :, :], g.merged[:, :, t * P:(t + 1) * P],
                                        m_hi[:, t % 2, :, :].bitcast(F32), ALU.subtract).then_inc(sem["m_lo"], 1)

            m_low(0)
            for n in range(4):
                dve.wait_ge(sem["w_hi"], n + 1)
                nc.vector.tensor_tensor(w_lo[:, 2 * n:2 * n + 2, :], b.unit("out", n),
                                        w_hi[:, 2 * n:2 * n + 2, :].bitcast(F32), ALU.subtract).then_inc(b.out_read, 1)
            m_low(1)
            dve.wait_ge(sem["rows_ready"], 3)
            for t in range(TT):
                x1t, h2t, st = x1[:, t % 2, :], h2[:, t % 2, :], stat[:, t % 2, :]
                dve.wait_ge(sem["mix_ps"], t + 1)
                if t >= 2:
                    dve.wait_ge(sem[f"stored_x1_{t % 2}"], 16 * (t // 2))
                dve.wait_ge(sem[f"x_in{t % 2}"], 16 * (t // 2 + 1))
                chain(nc.vector.tensor_tensor(x1t, mix(t), rows(0), ALU.mult))
                nc.vector.tensor_tensor(x1t, x1t, x[:, t % 2, :], ALU.add).then_inc(sem["x1_ready"], 1)
                if t + 2 < TT:
                    m_low(t + 2)
                dve.wait_ge(sem["std"], t + 1)
                chain(nc.vector.reciprocal(st[:, 2:3], st[:, 1:2]))
                chain(nc.vector.scalar_tensor_tensor(out=h2t, in0=x1t, scalar=st[:, 2:3], in1=rows(1),
                                                     op0=ALU.mult, op1=ALU.mult))
                nc.vector.tensor_tensor(h2t, h2t, rows(2), ALU.add).then_inc(sem["h2_ready"], 1)
                dve.wait_ge(sem["logit_ps"], t + 1)
                nc.vector.tensor_copy(logits[:, t % 4, t // 4, :], ps_log[:, 0:E]).then_inc(sem["logits"], 1)
            dve.wait_ge(sem["logits"], TT)
            chain(nc.vector.tensor_reduce(soft[:, 0, :], by_tile, AX.X, ALU.max))
            nc.vector.tensor_tensor(by_tile, by_tile, soft[:, 0, :].unsqueeze(2).to_broadcast([P, TT, E]),
                                    ALU.subtract).then_inc(sem["shifted"], 1)
            dve.wait_ge(sem["exped"], 1)
            chain(nc.vector.tensor_reduce(soft[:, 1, :], by_tile, AX.X, ALU.add))
            chain(nc.vector.reciprocal(soft[:, 2, :], soft[:, 1, :]))
            nc.vector.tensor_tensor(by_tile, by_tile, soft[:, 2, :].unsqueeze(2).to_broadcast([P, TT, E]),
                                    ALU.mult).then_inc(sem["affinity"], 1)
            dve.wait_ge(sem["aff_ready"], 1)
            for r in range(CAP // 8):
                eight = slice(8 * r, 8 * r + 8)
                chain(nc.vector.max(best[:, eight], aff))
                chain(nc.vector.max_index(best_at[:, eight], best[:, eight], aff))
                chain(nc.vector.match_replace(aff, best[:, eight], aff, -1.0))
            chain(nc.vector.tensor_copy(best_at_f, best_at[:, :]))
            chain(nc.vector.tensor_copy(best_up, best[:, ::-1]))
            nc.vector.tensor_copy(best_at_up, best_at_f[:, ::-1]).then_inc(sem["chosen"], 1)
            dve.wait_ge(sem["choice_ps"], 1)
            turned = ps_choice[:, 0:8 * E].rearrange("p (l h e) -> p l h e", h=2, e=E)
            early, early_at, late, late_at = turned[:, 0, 0, :], turned[:, 1, 0, :], turned[:, 2, 1, :], turned[:, 3, 1, :]
            chain(nc.vector.tensor_copy(pick[:, 0, :], early))
            chain(nc.vector.tensor_copy(pick[:, 1, :], early_at))
            chain(nc.vector.tensor_tensor(g.slot_gate[:, :], pick[:, 0, :], late, ALU.max))
            chain(nc.vector.tensor_tensor(pick[:, 0, :], pick[:, 0, :], late, ALU.is_ge))
            chain(nc.vector.scalar_tensor_tensor(out=pick[:, 1, :], in0=pick[:, 1, :], scalar=-float(T // 2), in1=late_at,
                                                 op0=ALU.add, op1=ALU.subtract))
            chain(nc.vector.tensor_tensor(pick[:, 1, :], pick[:, 1, :], pick[:, 0, :], ALU.mult))
            chain(nc.vector.scalar_tensor_tensor(out=g.slot_token[:, :], in0=pick[:, 1, :], scalar=float(T // 2),
                                                 in1=late_at, op0=ALU.add, op1=ALU.add))

        @block.tensor
        def _(pe):
            for r in range(3):
                if r >= 2:
                    pe.wait_ge(sem["rows_ready"], r - 1)
                for c in range(KC):
                    at = row_cols[r] + c
                    last = nc.tensor.matmul(mix(r)[:, c * P:(c + 1) * P], mod[:, at:at + 1].to_broadcast([P, P]), ident,
                                            start=True, stop=True)
                last.then_inc(sem["rows_ps"], 1)
            pe.wait_ge(sem["rows_ready"], 3)

            def router_of(t):
                pe.wait_ge(sem["h2_ready"], t + 1)
                if t:
                    pe.wait_ge(sem["tr_read"], t)
                for c in range(KC):
                    last = nc.tensor.transpose(flat_tr[:, c * P:(c + 1) * P], h2[:, t % 2, c * P:(c + 1) * P], ident)
                last.then_inc(sem["tr_ps"], 1)
                pe.wait_ge(sem["tr_read"], t + 1)
                if t:
                    pe.wait_ge(sem["logits"], t)
                for c in range(KC):
                    last = nc.tensor.matmul(ps_log[:, 0:E], h2_t[:, c, :], router[:, c, :],
                                            start=(c == 0), stop=(c == KC - 1))
                last.then_inc(sem["logit_ps"], 1)

            pe.wait_ge(sem["router_in"], 16)
            for t in range(TT):
                pe.wait_ge(sem["m_lo"], t + 1)
                if t >= 2:
                    pe.wait_ge(sem["x1_ready"], t - 1)
                for h in range(2):
                    for c in range(KC):
                        if t == 0 and h == 0 and c % 2 == 0:
                            pe.wait_ge(b.out_read, c // 2 + 1)
                        cols = slice(h * HALF, (h + 1) * HALF)
                        for m, (l, r) in enumerate(((m_hi, w_hi), (m_hi, w_lo), (m_lo, w_hi))):
                            last = nc.tensor.matmul(mix(t)[:, cols], l[:, t % 2, c, :], r[:, c, cols],
                                                    start=(c == 0 and m == 0), stop=(c == KC - 1 and m == 2))
                last.then_inc(sem["mix_ps"], 1)
                if t:
                    router_of(t - 1)
            router_of(TT - 1)
            pe.wait_ge(sem["affinity"], 1)
            pe.wait_ge(sem["tr_read"], TT)
            for t in range(4):
                last = nc.tensor.transpose(flat_tr[0:2 * E, t * P:(t + 1) * P],
                                           logits[:, t, :, :].rearrange("p b e -> p (b e)"), ident)
            last.then_inc(sem["aff_ps"], 1)
            pe.wait_ge(sem["chosen"], 1)
            for n in range(4):
                last = nc.tensor.transpose(ps_choice[:, 2 * E * n:2 * E * (n + 1)], lists[:, n, :],
                                           const[0:2 * E, C_ID:C_ID + 2 * E])
            last.then_inc(sem["choice_ps"], 1)


TILES = [("gate", 0), ("up", 0), ("gate", 1), ("up", 1), ("gate", 2), ("up", 2), ("down", 0),
         ("gate", 3), ("up", 3), ("down", 1), ("down", 2), ("down", 3)]
NT = len(TILES)
QUARTER = FF // 4
TILE = KC * QUARTER
RAW_TILES = 4
TURNS = {2: 0, 4: 1, 7: 2, 8: "x", 9: 3}
TURN_ORDER = [0, 1, 2, "x", 3]


def stage_experts(b, g, out, h2_dram):
    nc, d = b.nc, b.dram
    with ExitStack() as ctx:
        raw = b.sb("moe_raw", [P, RAW_TILES, TILE], ctx=ctx)
        w_hi, w_lo = b.sb("moe_w_hi", [P, 2, TILE], F32R, ctx), b.sb("moe_w_lo", [P, 2, TILE], F32R, ctx)
        x = b.sb("moe_x", [P, D], ctx=ctx)
        x_hi, x_lo = b.sb("moe_x_hi", [P, KC, P], F32R, ctx), b.sb("moe_x_lo", [P, KC, P], F32R, ctx)
        silu, hidden = b.sb("moe_silu", [P, QUARTER], ctx=ctx), b.sb("moe_hidden", [P, QUARTER], ctx=ctx)
        h_hi, h_lo = b.sb("moe_h_hi", [P, 4, 4, P], F32R, ctx), b.sb("moe_h_lo", [P, 4, 4, P], F32R, ctx)
        y, gate2 = b.sb("moe_y", [P, D], ctx=ctx), b.sb("moe_gate2", [P, D], ctx=ctx)
        gate_at = b.sb("gate_at", [P, 1], ctx=ctx)
        ps_gu, ps_down, ps_turn = b.ps("ps_gu", [P, 4, HALF], ctx), b.ps("ps_down", [P, 2, HALF], ctx), b.ps("ps_turn", [P, 2, HALF], ctx)
        tile_in = [b.sem(f"moe_tile_in{s}") for s in range(RAW_TILES)]
        hi_ready, lo_ready = b.sem("moe_hi_ready"), b.sem("moe_lo_ready")
        tile_done = b.sem("moe_tile_done")
        silu_ready, hidden_ready = b.sem("moe_silu_ready"), b.sem("moe_hidden_ready")
        turned, turn_hi, turn_lo = b.sem("moe_turned"), b.sem("moe_turn_hi"), b.sem("moe_turn_lo")
        gathered, scattered = b.sem("moe_gathered"), b.sem("moe_scattered")
        gate_set, down_begun = b.sem("moe_gate_set"), b.sem("moe_down_begun")
        y_ready, gate2_ps, gate2_ready = b.sem("moe_y_ready"), b.sem("moe_gate2_ps"), b.sem("moe_gate2_ready")
        block = ctx.enter_context(nc.Block())
        ident = g.const[:, C_ID:C_ID + P]
        flat_turn = ps_turn[:, :, :].rearrange("p a n -> p (a n)")
        flat_down = ps_down[:, :, :].rearrange("p a n -> p (a n)")
        gate_bank = lambda q: ps_gu[:, 2 * (q % 2), :]
        up_bank = lambda q: ps_gu[:, 2 * (q % 2) + 1, :]
        at = {name: t for t, name in enumerate(TILES)}

        def half(ring, slot, i):
            return ring[:, slot, i * TILE // 2:(i + 1) * TILE // 2]

        def turn_view(what):
            if what == "x":
                return flat_turn, x_hi[:, :, :].rearrange("p c n -> p (c n)"), x_lo[:, :, :].rearrange("p c n -> p (c n)")
            return (ps_turn[:, what % 2, :], h_hi[:, what, :, :].rearrange("p c n -> p (c n)"),
                    h_lo[:, what, :, :].rearrange("p c n -> p (c n)"))

        turns_before = lambda e, what: e * 5 + 1 + TURN_ORDER.index(what)

        @block.sync
        def _(sp):
            def fetch(e, t, tiles_split=None):
                kind, q = TILES[t]
                w = d["w_" + kind][0][e]
                if kind == "down":
                    src = w.rearrange("(q c p) n -> q p c n", q=4, p=P)[q]
                    dst = raw[:, t % RAW_TILES, :].rearrange("p (c n) -> p c n", n=D)
                else:
                    src = w.rearrange("(c p) (q n) -> q p c n", p=P, q=4)[q]
                    dst = raw[:, t % RAW_TILES, :].rearrange("p (c n) -> p c n", n=QUARTER)
                if tiles_split is not None:
                    sp.wait_ge(lo_ready, 2 * tiles_split)
                sp.dma_start(dst, src).then_inc(tile_in[t % RAW_TILES], 16)

            for t in range(RAW_TILES):
                fetch(0, t)

            def expert(e, last=False):
                for t in range(RAW_TILES, NT if last else NT + RAW_TILES):
                    split = e * NT + t - RAW_TILES + 1
                    if t == TILES.index(("down", 0)):
                        sp.wait_ge(lo_ready, 2 * split)
                        sp.sem_inc(down_begun, 1)
                        split = None
                    fetch(e if t < NT else e + 1, t % NT, split)

            with sp.Fori(0, E - 1) as e:
                expert(e)
            expert(E - 1, last=True)

        @block.scalar
        def _(act):
            def high(e, t):
                act.wait_ge(tile_in[t % RAW_TILES], e * (16 * NT // RAW_TILES) + 16 * (t // RAW_TILES + 1))
                if t >= 2:
                    act.wait_ge(tile_done, e * NT + t - 1)
                for i in range(2):
                    nc.scalar.activation(half(w_hi, t % 2, i), half(raw, t % RAW_TILES, i), ACT.Copy).then_inc(hi_ready, 1)

            def turn(count, what):
                src, hi, _ = turn_view(what)
                act.wait_ge(turned, count)
                nc.scalar.activation(hi, src, ACT.Copy).then_inc(turn_hi, 1)

            act.wait_ge(gate2_ps, 1)
            nc.scalar.activation(gate2[:, :], flat_down, ACT.Copy).then_inc(gate2_ready, 1)
            turn(1, "x")
            high(0, 0)
            high(0, 1)

            def expert(e, last=False):
                for t, (kind, q) in enumerate(TILES):
                    if not last or t + 2 < NT:
                        high(e, t + 2)
                    if t in TURNS and not (last and TURNS[t] == "x"):
                        count = turns_before(e, TURNS[t]) + 1
                        turn(count - 1 if last and t > 8 else count, TURNS[t])
                    if kind == "gate":
                        act.wait_ge(tile_done, e * NT + t + 1)
                        nc.scalar.activation(silu[:, :], gate_bank(q), ACT.Silu).then_inc(silu_ready, 1)

            with act.Fori(0, E - 1) as e:
                expert(e)
            expert(E - 1, last=True)

        @block.vector
        def _(dve):
            def low(e, t):
                for i in range(2):
                    dve.wait_ge(hi_ready, e * (2 * NT) + 2 * t + i + 1)
                    nc.vector.tensor_tensor(half(w_lo, t % 2, i), half(raw, t % RAW_TILES, i),
                                            half(w_hi, t % 2, i).bitcast(F32), ALU.subtract).then_inc(lo_ready, 1)

            def turn(count, what):
                src, hi, lo = turn_view(what)
                dve.wait_ge(turn_hi, count)
                nc.vector.tensor_tensor(lo, src, hi.bitcast(F32), ALU.subtract).then_inc(turn_lo, 1)

            turn(1, "x")
            low(0, 0)
            low(0, 1)

            def expert(e, last=False):
                for t, (kind, q) in enumerate(TILES):
                    if kind == "up":
                        dve.wait_ge(tile_done, e * NT + t + 1)
                        dve.wait_ge(silu_ready, e * 4 + q + 1)
                        nc.vector.tensor_tensor(hidden[:, :], silu[:, :], up_bank(q), ALU.mult).then_inc(hidden_ready, 1)
                    if not last or t + 2 < NT:
                        low(e, t + 2)
                    if t in TURNS and not (last and TURNS[t] == "x"):
                        count = turns_before(e, TURNS[t]) + 1
                        turn(count - 1 if last and t > 8 else count, TURNS[t])
                dve.wait_ge(tile_done, e * NT + NT)
                dve.wait_ge(gate_set, e + 1)
                for i in range(2):
                    cols = slice(i * HALF, (i + 1) * HALF)
                    nc.vector.scalar_tensor_tensor(out=y[:, cols], in0=ps_down[:, i, :], scalar=gate_at[:, 0:1],
                                                   in1=gate2[:, cols], op0=ALU.mult, op1=ALU.mult
                                                   ).then_inc(y_ready, 1)

            dve.wait_ge(gate2_ready, 1)
            with dve.Fori(0, E - 1) as e:
                expert(e)
            expert(E - 1, last=True)

        @block.gpsimd
        def _(pool):
            def gather(e):
                nc.gpsimd.indirect_dma_start(x[:, :], None, h2_dram,
                                             bass.IndirectOffsetOnAxis(g.slot_token[:, e:e + 1], 0)
                                             ).then_inc(gathered, 16)

            gather(0)
            for e in range(E):
                nc.gpsimd.tensor_copy(gate_at[:, :], g.slot_gate[:, e:e + 1]).then_inc(gate_set, 1)
                if e + 1 < E:
                    pool.wait_ge(turned, 5 * e + 1)
                    gather(e + 1)
                pool.wait_ge(y_ready, 2 * e + 2)
                nc.gpsimd.indirect_dma_start(out[0], bass.IndirectOffsetOnAxis(g.slot_token[:, e:e + 1], 0),
                                             y[:, :], None, compute_op=ALU.add).then_inc(scattered, 16)
                pool.wait_ge(scattered, 16 * e + 16)

        @block.tensor
        def _(pe):
            for c in range(KC):
                last_mm = nc.tensor.matmul(flat_down[:, c * P:(c + 1) * P], g.mod[:, 40 + c:41 + c].to_broadcast([P, P]), ident,
                                           start=True, stop=True)
            last_mm.then_inc(gate2_ps, 1)

            def turn(what):
                src, n = (x, KC) if what == "x" else (hidden, 4)
                dst = turn_view(what)[0]
                for c in range(n):
                    ins = nc.tensor.transpose(dst[:, c * P:(c + 1) * P], src[:, c * P:(c + 1) * P], ident)
                ins.then_inc(turned, 1)

            def product(bank, lhs_hi, lhs_lo, t, c, cols, start, stop):
                for m, (a, w) in enumerate(((lhs_hi, w_hi), (lhs_hi, w_lo), (lhs_lo, w_hi))):
                    ins = nc.tensor.matmul(bank, a, w[:, t % 2, cols], start=start and m == 0, stop=stop and m == 2)
                return ins

            pe.wait_ge(gathered, 16)
            turn("x")
            pe.wait_ge(gate2_ready, 1)

            def expert(e, last=False):
                pe.wait_ge(turn_lo, e * 5 + 1)
                for t, (kind, q) in enumerate(TILES):
                    if kind == "down":
                        pe.wait_ge(turn_lo, (e * 5 + 5) if last and q == 3 else turns_before(e, q) + 1)
                        if q == 0:
                            pe.wait_ge(gate_set, e + 1)
                    for i in range(2):
                        pe.wait_ge(lo_ready, e * (2 * NT) + 2 * t + i + 1)
                        if kind == "down":
                            for c in range(2 * i, 2 * i + 2):
                                for n in range(2):
                                    ins = product(ps_down[:, n, :], h_hi[:, q, c, :], h_lo[:, q, c, :], t, c,
                                                  slice(c * D + n * HALF, c * D + (n + 1) * HALF),
                                                  q == 0 and c == 0, q == 3 and c == 3)
                        else:
                            bank = gate_bank(q) if kind == "gate" else up_bank(q)
                            for c in range(4 * i, 4 * i + 4):
                                ins = product(bank, x_hi[:, c, :], x_lo[:, c, :], t, c,
                                              slice(c * QUARTER, (c + 1) * QUARTER), c == 0, c == KC - 1)
                    ins.then_inc(tile_done, 1)
                    if t in TURNS:
                        what = TURNS[t]
                        if what == "x":
                            if last:
                                continue
                            pe.wait_ge(gathered, e * 16 + 32)
                            pe.wait_ge(turn_lo, turns_before(e, "x"))
                        else:
                            pe.wait_ge(hidden_ready, e * 4 + what + 1)
                            if what == 3:
                                pe.wait_ge(turn_lo, (e * 5 + 4) if last else turns_before(e, 3))
                        turn(what)

            with pe.Fori(0, E - 1) as e:
                expert(e)
            expert(E - 1, last=True)


class Shared:
    pass


INPUTS = ["x", "c", "positions", "w_ada", "b_ada", "norm1_w", "w_in", "q_norm_w", "k_norm_w", "conv_w",
          "conv_b", "lru_w_a", "lru_b_a", "lru_w_x", "lru_b_x", "lru_lambda", "w_attn_branch",
          "w_lru_branch", "w_out", "norm2_w", "w_router", "w_gate", "w_up", "w_down", "const"]


def program(nc, dram, out, debug=None):
    with ExitStack() as ctx:
        b = Build(nc, ctx, dram)
        g = Shared()
        g.const = b.sb("const", [P, C_END])
        g.par_a, g.par_b = b.sb("par_a", [P, A_END]), b.sb("par_b", [P, B_END])
        g.mod, g.cact, g.acc = b.sb("mod", [P, 48]), b.sb("silu_c", [P, KC]), b.sb("acc", [P, 2, UNIT])
        g.acc_free = b.sem("acc_free")
        g.slot_gate, g.slot_token = b.sb("slot_gate", [P, E]), b.sb("slot_token", [P, E], U32)
        with ExitStack() as mixer:
            b.rings(mixer)
            g.h_hi = b.sb("h_hi", [P, KC, T], F32R, mixer)
            g.h_lo = b.sb("h_lo", [P, KC, T], F32R, mixer)
            g.attn_t = b.sb("attn_t", [P, 2, T], ctx=mixer)
            stage_norm(b, g)
            with ExitStack() as qkv:
                g.q = b.sb("q", [P, QK_CHUNKS, T], ctx=qkv)
                g.k = b.sb("k", [P, QK_CHUNKS, T], ctx=qkv)
                g.v = b.sb("v", [P, GROUPS, TT, UNIT], ctx=qkv)
                stage_qkv(b, g)
                stage_attention(b, g)
            g.lru_t = b.sb("lru_t", [P, KC, T], ctx=mixer)
            stage_lru(b, g)
            g.merged = b.sb("merged", [P, KC, T], ctx=mixer)
            stage_merge(b, g)
            if debug: debug("merge", b, g)
            h2_dram = nc.dram_tensor("h2_rows", (T, D), F32).ap()
            stage_out(b, g, out, h2_dram)
            if debug: debug("out", b, g)
        stage_experts(b, g, out, h2_dram)
        if debug: debug("end", b, g)


def kernel(**inputs):
    import concourse.bacc as bacc
    from concourse.bass_utils import run_bass_kernel_spmd

    nc = bacc.Bacc("TRN2", target_bir_lowering=False, num_devices=1)
    arrays, dram = {}, {}
    for name in INPUTS:
        a = constants() if name == "const" else np.ascontiguousarray(inputs[name])
        arrays[f"in_{name}"] = a
        dram[name] = nc.dram_tensor(f"in_{name}", a.shape, mybir.dt.from_np(a.dtype), kind="ExternalInput").ap()
    out = nc.dram_tensor("out_x", (1, T, D), F32, kind="ExternalOutput").ap()
    program(nc, dram, out)
    r = run_bass_kernel_spmd(nc, [arrays], core_ids=[0])
    return r.results[0]["out_x"]
```

```python
from contextlib import ExitStack

import numpy as np

import concourse.bass as bass
from concourse import mybir

P = 128
F32 = mybir.dt.float32
F32R = mybir.dt.float32r
I32 = mybir.dt.int32
U32 = mybir.dt.uint32
ALU = mybir.AluOpType
ACT = mybir.ActivationFunctionType
AX = mybir.AxisListType

D = 1024
T = 1024
KC = D // P
TT = T // P
HALF = 512
HD = 64
GROUPS = 3
ROWS = 32
SLOTS = 4
AW = GROUPS * SLOTS * HD
QK_CHUNKS = AW // P
E = 16
FF = 2 * D
CAP = 2 * T // E
EPS = 1e-6
NEG = -1e30
UNIT = 256
RAW = 3
IN_Q, IN_K, IN_V = 0, AW, 2 * AW
IN_XR = 3 * AW
IN_YR = IN_XR + D
IN_GA = IN_YR + D
IN_GL = IN_GA + D
G0_KEYS, G12_KEYS = 640, 256
KEYS = G0_KEYS + 2 * G12_KEYS
M0_PAD = P + 3
CONV = 4

C_ID = 0
C_ONE = C_ID + P
C_EPS = C_ONE + 1
C_SEL = C_EPS + 1
C_SIGN = C_SEL + 2 * ROWS - 2
C_M0 = C_SIGN + 1
C_M1 = C_M0 + G0_KEYS + M0_PAD + 1
C_M2 = C_M1 + G12_KEYS + P
C_FREQ = C_M2 + G12_KEYS
C_PI2 = C_FREQ + 1
C_END = C_PI2 + 1

A_C, A_N1, A_N2, A_QN, A_KN, A_BADA = 0, 8, 16, 24, 30, 36
A_END = A_BADA + 48
B_CW, B_CB, B_BA, B_BX, B_LAM = 0, 32, 40, 56, 72
B_END = 88


def constants():
    c = np.zeros((P, C_END), np.float32)
    p = np.arange(P)
    c[:, C_ID:C_ID + P] = np.eye(P)
    c[:, C_ONE] = 1.0
    c[:, C_SEL + ROWS - 2:C_SEL + ROWS] = (p[:, None] // HD == np.arange(2)[None, :]) / HD
    half = HD // 2
    c[:, C_SIGN] = np.where(p % HD < half, -1.0, 1.0)
    y = np.arange(G0_KEYS + M0_PAD + 1)
    c[:, C_M0:C_M1] = np.where(np.abs(y[None] - M0_PAD - 4 * p[:, None]) <= 64, 0.0, NEG)
    y = np.arange(G12_KEYS + P)
    c[:, C_M1:C_M2] = np.where(np.abs(y[None] - P - p[:, None]) <= 64, 0.0, NEG)
    y = np.arange(G12_KEYS)
    c[:, C_M2:C_FREQ] = np.where((y[None] - p[:, None]) % 4 == 0, 0.0, NEG)
    inv = np.float32(10000.0) ** (-np.arange(half, dtype=np.float32) / np.float32(half))
    c[:, C_FREQ] = inv[p % half]
    c[:, C_EPS] = EPS
    c[:, C_PI2] = np.pi / 2
    return c


def fetch_plan():
    plan = [("ada", u, "dve") for u in range(8)]
    ada = lambda u: ("ada", u, "dve")
    plan += [("qk", 0, "dve"), ada(8)]
    for n in range(1, 6):
        plan += [("qk", n, "dve"), ada(7 + 2 * n), ada(8 + 2 * n)]
    plan += [("v", 0, "dve"), ada(19), ada(20), ("v", 1, "dve"), ada(21), ("v", 2, "dve"), ada(22), ada(23)]
    plan += [("xy", n, "dve") for n in range(KC)]
    plan += [("ga", 0, "dve")] + [("lru", n, "dve") for n in range(8)] + [("gl", 0, "dve"), ("attn", 0, "pe")]
    for n in range(1, 4):
        plan += [("ga", n, "dve"), ("gl", n, "dve"), ("attn", n, "pe")]
    plan += [("out", n, "dve") for n in range(4)]
    return plan


class Build:

    def __init__(self, nc, ctx, dram):
        self.nc, self.ctx, self.dram = nc, ctx, dram
        self.plan = fetch_plan()
        self.order = {(k, n): u for u, (k, n, _) in enumerate(self.plan)}
        split_kinds = ("qk", "v", "xy", "ga", "gl", "lru", "out")
        self.items = {}
        counts = {"ada": 0, "split": 0, "pe": 0}
        self.freed_by = []
        for kind, n, reader in self.plan:
            group = "ada" if kind == "ada" else "split" if kind in split_kinds else "pe"
            if group == "split":
                self.items[(kind, n)] = 2 * counts["split"]
            counts[group] += 1
            self.freed_by.append((group, counts[group]))
        self.raw_in = [self.sem(f"raw_in{s}") for s in range(RAW)]
        self.ada_read = self.sem("ada_read")
        self.raw_pe = self.sem("raw_pe")
        self.hi_ready = self.sem("hi_ready")
        self.split_ready = self.sem("split_ready")
        self.pair_done = self.sem("pair_done")
        self.out_hi = self.sem("out_hi")
        self.out_read = self.sem("out_read")
        self.issued = 0

    def rings(self, ctx, place):
        self.raw = place.rearrange("p (s n) -> p s n", s=RAW)
        self.hi = self.sb("hi_ring", [P, 2, D], F32R, ctx)
        self.lo = self.sb("lo_ring", [P, 2, D], F32R, ctx)

    def sb(self, name, shape, dt=F32, ctx=None):
        return (ctx or self.ctx).enter_context(self.nc.sbuf_tensor(name, shape, dt))

    def ps(self, name, shape, ctx):
        return ctx.enter_context(self.nc.psum_tensor(name, shape, F32))

    def sem(self, name):
        return self.ctx.enter_context(self.nc.semaphore(name))

    def source(self, kind, n):
        d = self.dram
        w_in = d["w_in"][0].rearrange("(c p) n -> p c n", p=P)
        rows = lambda w: w.rearrange("(c p) n -> p c n", p=P)
        cols = lambda w, start: w[:, :, start:start + UNIT]
        if kind == "ada":
            return cols(rows(d["w_ada"][0]), n * UNIT)
        if kind == "qk":
            return cols(w_in, (IN_Q if n < 3 else IN_K) + (n % 3) * UNIT)
        if kind == "xy":
            return [w_in[:, :, start + n * P:start + (n + 1) * P] for start in (IN_XR, IN_YR)]
        if kind in ("v", "ga", "gl"):
            start = {"v": IN_V, "ga": IN_GA, "gl": IN_GL}[kind]
            return cols(w_in, start + n * UNIT)
        if kind == "lru":
            return rows(d["w_lru_branch"][0])[:, 4 * (n % 2):4 * (n % 2) + 4, n // 4 * HALF:(n // 4 + 1) * HALF]
        if kind == "attn":
            return cols(rows(d["w_attn_branch"][0]), n * UNIT)
        return rows(d["w_out"][0])[:, 2 * n:2 * n + 2, :]

    def unit(self, kind, n):
        s = self.order[(kind, n)] % RAW
        if kind == "out":
            return self.raw[:, s, :].rearrange("p (c n) -> p c n", c=2)
        if kind == "lru":
            return self.raw[:, s, :].rearrange("p (c n) -> p c n", c=4)
        c = 2 if kind == "attn" else KC
        return self.raw[:, s, 0:c * UNIT].rearrange("p (c n) -> p c n", c=c)

    def fetch_until(self, sp, kind, n):
        self.fetch_count(sp, min(self.order[(kind, n)] + RAW + 1, len(self.plan)))

    def fetch_count(self, sp, total):
        while self.issued < total:
            u = self.issued
            k, m, _ = self.plan[u]
            if u >= RAW:
                group, count = self.freed_by[u - RAW]
                if group == "ada":
                    sp.wait_ge(self.ada_read, count)
                elif k == "out" and self.plan[u - RAW][0] == "out":
                    sp.wait_ge(self.out_read, 1)
                elif group == "split":
                    sp.wait_ge(self.split_ready, 2 * count)
                else:
                    sp.wait_ge(self.raw_pe, count)
            if k == "xy":
                for i, src in enumerate(self.source(k, m)):
                    sp.dma_start(self.item(k, m, i), src).then_inc(self.raw_in[u % RAW], 16)
            else:
                sp.dma_start(self.unit(k, m), self.source(k, m)).then_inc(self.raw_in[u % RAW], 16)
            self.issued += 1

    def arrived(self, eng, kind, n):
        u = self.order[(kind, n)]
        fetches = sum(2 if k == "xy" else 1 for k, _, _ in self.plan[u % RAW:u + 1:RAW])
        eng.wait_ge(self.raw_in[u % RAW], 16 * fetches)

    def item(self, kind, n, i):
        raw = self.unit(kind, n)
        if kind == "xy":
            s = self.order[(kind, n)] % RAW
            return self.raw[:, s, i * D:(i + 1) * D].rearrange("p (c n) -> p c n", c=KC)
        if kind == "v":
            return raw[:, 4 * i:4 * i + 4, :]
        if kind == "lru":
            return raw[:, 2 * i:2 * i + 2, :]
        if kind == "out":
            return raw[:, i, :]
        return raw[:, :, i * P:(i + 1) * P]

    def shaped(self, ring, kind, slot):
        if kind == "v":
            return ring[:, slot, :].rearrange("p (c n) -> p c n", c=4)
        if kind == "lru":
            return ring[:, slot, :].rearrange("p (c n) -> p c n", c=2)
        if kind == "out":
            return ring[:, slot, :]
        return ring[:, slot, :].rearrange("p (c n) -> p c n", c=KC)

    def split_high(self, act, kind, n, i):
        k = self.items[(kind, n)] + i
        self.arrived(act, kind, n)
        if k >= 2:
            act.wait_ge(self.pair_done, k - 1)
        self.nc.scalar.activation(self.shaped(self.hi, kind, k % 2), self.item(kind, n, i),
                                  ACT.Copy).then_inc(self.hi_ready, 1)

    def split_low(self, dve, kind, n, i):
        k = self.items[(kind, n)] + i
        dve.wait_ge(self.hi_ready, k + 1)
        self.nc.vector.tensor_tensor(self.shaped(self.lo, kind, k % 2), self.item(kind, n, i),
                                     self.shaped(self.hi, kind, k % 2).bitcast(F32),
                                     ALU.subtract).then_inc(self.split_ready, 1)

    def project(self, out2, kind, n, i, moving_hi, moving_lo):
        k = self.items[(kind, n)] + i
        self.nc.tensor.wait_ge(self.split_ready, k + 1)
        whi, wlo = (self.shaped(r, kind, k % 2) for r in (self.hi, self.lo))
        for half in range(2):
            cols = slice(half * HALF, (half + 1) * HALF)
            for c in range(KC):
                for w, a in ((whi, moving_hi), (whi, moving_lo), (wlo, moving_hi)):
                    last = self.nc.tensor.matmul(out2[:, cols], w[:, c, :], a[:, c, cols],
                                                 start=(c == 0 and w is whi and a is moving_hi),
                                                 stop=(c == KC - 1 and w is wlo))
        last.then_inc(self.pair_done, 1)
        return last


class Chain:

    def __init__(self, eng, sem):
        self.eng, self.sem, self.n = eng, sem, 0

    def __call__(self, instruction):
        instruction.then_inc(self.sem, 1)
        self.n += 1
        self.eng.wait_ge(self.sem, self.n)


def out_high(b, act, g, n):
    b.arrived(act, "out", n)
    b.nc.scalar.activation(g.h_hi[:, 2 * n:2 * n + 2, :], b.unit("out", n), ACT.Copy).then_inc(b.out_hi, 1)


def out_low(b, dve, g, n):
    dve.wait_ge(b.out_hi, n + 1)
    b.nc.vector.tensor_tensor(g.h_lo[:, 2 * n:2 * n + 2, :], b.unit("out", n),
                              g.h_hi[:, 2 * n:2 * n + 2, :].bitcast(F32), ALU.subtract).then_inc(b.out_read, 1)


def ada_unit(b, dve, chain, u, acc, acc_free, cact):
    b.arrived(dve, "ada", u)
    if u >= 2:
        dve.wait_ge(acc_free, u - 1)
    w = b.unit("ada", u)
    a = acc[:, u % 2, :]
    chain(b.nc.vector.tensor_scalar(a, w[:, 0, :], cact[:, 0:1], None, ALU.mult))
    for c in range(1, KC):
        ins = b.nc.vector.scalar_tensor_tensor(out=a, in0=w[:, c, :], scalar=cact[:, c:c + 1], in1=a,
                                               op0=ALU.mult, op1=ALU.add)
        if c < KC - 1:
            chain(ins)
    ins.then_inc(b.ada_read, 1)


def ada_sum(b, pe, u, acc, acc_free, ps_mod, ones_col):
    pe.wait_ge(b.ada_read, u + 1)
    for i in range(2):
        last = b.nc.tensor.matmul(ps_mod[:, 2 * u + i:2 * u + i + 1], acc[:, u % 2, i * P:(i + 1) * P],
                                  ones_col, start=True, stop=True)
    last.then_inc(acc_free, 1)


def stage_norm(b, g):
    nc, d = b.nc, b.dram
    with ExitStack() as ctx:
        x_in = [b.sem(f"x_in{i}") for i in range(2)]
        rows_in, const_in, rest_in = b.sem("rows_in"), b.sem("const_in"), b.sem("const_rest_in")
        c_in, c_ps, rstd_ready = b.sem("c_in"), b.sem("c_ps"), b.sem("rstd_ready")
        par_ps, par_ready, silu_ready = b.sem("par_ps"), b.sem("par_ready"), b.sem("silu_ready")
        squares, std_ready, xn_ready = b.sem("squares"), b.sem("std_ready"), b.sem("xn_ready")
        xt_ps, h_hi, h_lo = b.sem("xt_ps"), b.sem("h_hi"), b.sem("h_lo")
        h32_dve, h32_act, mod_ready = b.sem("h32_dve"), b.sem("h32_act"), b.sem("mod1_ready")
        link = b.sem("norm_link")
        rows_a = b.sb("rows_a", [A_END, P], ctx=ctx)
        rows_b = b.sb("rows_b", [B_END, P], ctx=ctx)
        x = g.area[:, 0:TT * D].rearrange("p (t n) -> p t n", n=D)
        scratch = b.sb("square_scratch", [P, D], ctx=ctx)
        ss = b.sb("sum_squares", [P, TT], ctx=ctx)
        std = b.sb("std", [P, TT], ctx=ctx)
        rstd = b.sb("rstd", [P, TT], ctx=ctx)
        h32 = b.sb("h32", [P, 4, HALF], ctx=ctx)
        ps_par = b.ps("ps_par", [P, HALF], ctx)
        ps_mod = b.ps("ps_mod0", [P, HALF], ctx)
        ps_x = b.ps("ps_x", [P, 4, HALF], ctx)
        const, par_a, par_b, mod, cact, acc = g.const, g.par_a, g.par_b, g.mod, g.cact, g.acc
        x_dram = d["x"][0].rearrange("(t p) n -> p t n", p=P)
        block = ctx.enter_context(nc.Block())

        @block.sync
        def _(sp):
            sp.dma_start(const[:, 0:C_SEL], d["const"][:, 0:C_SEL]).then_inc(const_in, 16)
            b.fetch_count(sp, 2)
            sp.dma_start(x[:, 0:4, :], x_dram[:, 0:4, :]).then_inc(x_in[0], 16)
            b.fetch_count(sp, 5)
            sp.dma_start(x[:, 4:8, :], x_dram[:, 4:8, :]).then_inc(x_in[1], 16)
            b.fetch_count(sp, 7)
            sp.dma_start(const[:, C_SEL:], d["const"][:, C_SEL:]).then_inc(rest_in, 16)
            b.fetch_until(sp, "ada", 7)

        @block.scalar
        def _(act):
            rows = lambda ap: ap.rearrange("(r p) -> r p", p=P)
            parts = [(rows_a, A_N1, d["norm1_w"][0]), (rows_a, A_N2, d["norm2_w"][0]),
                     (rows_a, A_QN, d["q_norm_w"][0].rearrange("h n -> (h n)")),
                     (rows_a, A_KN, d["k_norm_w"][0].rearrange("h n -> (h n)")),
                     (rows_a, A_BADA, d["b_ada"][0]),
                     (rows_b, B_CW, d["conv_w"][0].rearrange("w o n -> (w o n)")), (rows_b, B_CB, d["conv_b"][0]),
                     (rows_b, B_BA, d["lru_b_a"][0].rearrange("w n -> (w n)")),
                     (rows_b, B_BX, d["lru_b_x"][0].rearrange("w n -> (w n)")),
                     (rows_b, B_LAM, d["lru_lambda"][0].rearrange("w n -> (w n)"))]
            act.dma_start(rows_a[A_C:A_C + KC, :], rows(d["c"][0])).then_inc(c_in, 16)
            act.wait_ge(c_ps, 1)
            nc.scalar.activation(cact[:, :], ps_par[:, 2 * P:2 * P + KC], ACT.Silu).then_inc(silu_ready, 1)
            for tile, at, ap in parts:
                n = ap.shape[0] // P
                act.dma_start(tile[at:at + n, :], rows(ap)).then_inc(rows_in, 16)
            for t in range(TT):
                if t % 4 == 0:
                    act.wait_ge(x_in[t // 4], 16)
                if t:
                    act.wait_ge(squares, t)
                nc.scalar.activation(scratch[:, :], x[:, t, :], ACT.Square,
                                     accum_out=ss[:, t:t + 1]).then_inc(squares, 1)
            act.wait_ge(squares, TT)
            nc.scalar.activation(std[:, :], ss[:, :], ACT.Sqrt, scale=1.0 / D,
                                 bias=const[:, C_EPS:C_EPS + 1]).then_inc(std_ready, 1)
            act.wait_ge(rstd_ready, 1)
            for t in range(TT):
                nc.scalar.activation(x[:, t, :], x[:, t, :], ACT.Identity, scale=rstd[:, t:t + 1]).then_inc(xn_ready, 1)
            for i in range(2):
                b.split_high(act, "qk", 0, i)
            act.wait_ge(mod_ready, 1)
            for j in range(0, 2 * KC, 2):
                c = j // 2
                act.wait_ge(xt_ps, j + 2)
                if j >= 4:
                    act.wait_ge(h_lo, j - 2)
                nc.scalar.activation(h32[:, (j + 1) % 4, :], ps_x[:, (j + 1) % 4, :], ACT.Identity,
                                     scale=mod[:, 8 + c:9 + c], bias=mod[:, c:c + 1]).then_inc(h32_act, 1)
                act.wait_ge(h32_dve, c + 1)
                nc.scalar.activation(g.h_hi[:, c, 0:HALF], h32[:, j % 4, :], ACT.Copy).then_inc(h_hi, 1)
                act.wait_ge(h32_act, c + 1)
                nc.scalar.activation(g.h_hi[:, c, HALF:T], h32[:, (j + 1) % 4, :], ACT.Copy).then_inc(h_hi, 1)

        def low(dve, j):
            c, cols = j // 2, slice(j % 2 * HALF, (j % 2 + 1) * HALF)
            dve.wait_ge(h_hi, j + 1)
            nc.vector.tensor_tensor(g.h_lo[:, c, cols], h32[:, j % 4, :], g.h_hi[:, c, cols].bitcast(F32),
                                    ALU.subtract).then_inc(h_lo, 1)

        @block.vector
        def _(dve):
            chain = Chain(dve, link)
            dve.wait_ge(silu_ready, 1)
            for u in range(8):
                ada_unit(b, dve, chain, u, acc, g.acc_free, cact)
                if u == 5:
                    dve.wait_ge(std_ready, 1)
                    nc.vector.reciprocal(rstd[:, :], std[:, :]).then_inc(rstd_ready, 1)
            dve.wait_ge(par_ps, 1)
            nc.vector.tensor_copy(par_a[:, :], ps_par[:, 0:A_END]).then_inc(par_ready, 1)
            nc.vector.tensor_copy(par_b[:, :], ps_par[:, P:P + B_END]).then_inc(par_ready, 1)
            for i in range(2):
                b.split_low(dve, "qk", 0, i)
            dve.wait_ge(rest_in, 16)
            dve.wait_ge(par_ready, 2)
            dve.wait_ge(g.acc_free, 8)
            chain(nc.vector.tensor_tensor(mod[:, 0:16], ps_mod[:, 0:16], par_a[:, A_BADA:A_BADA + 16], ALU.add))
            nc.vector.scalar_tensor_tensor(out=mod[:, 8:16], in0=mod[:, 8:16], scalar=1.0, in1=par_a[:, A_N1:A_N1 + 8],
                                           op0=ALU.add, op1=ALU.mult).then_inc(mod_ready, 1)
            dve.wait_ge(mod_ready, 1)

            def modulate(c):
                j = 2 * c
                dve.wait_ge(xt_ps, j + 1)
                if j >= 4:
                    dve.wait_ge(h_lo, j - 3)
                nc.vector.tensor_scalar(h32[:, j % 4, :], ps_x[:, j % 4, :], mod[:, 8 + c:9 + c],
                                        mod[:, c:c + 1], ALU.mult, ALU.add).then_inc(h32_dve, 1)

            modulate(0)
            for c in range(KC):
                if c + 1 < KC:
                    modulate(c + 1)
                dve.wait_ge(h32_dve, c + 1)
                low(dve, 2 * c)
                low(dve, 2 * c + 1)

        @block.tensor
        def _(pe):
            pe.wait_ge(const_in, 16)
            pe.wait_ge(c_in, 16)
            nc.tensor.transpose(ps_par[:, 2 * P:2 * P + KC], rows_a[A_C:A_C + KC, :],
                                const[0:KC, C_ID:C_ID + KC]).then_inc(c_ps, 1)
            for u in range(6):
                ada_sum(b, pe, u, acc, g.acc_free, ps_mod, const[:, C_ONE:C_ONE + 1])
            pe.wait_ge(rows_in, 16 * 10)
            pe.wait_ge(silu_ready, 1)
            nc.tensor.transpose(ps_par[:, 0:A_END], rows_a[:, :], const[0:A_END, C_ID:C_ID + A_END])
            nc.tensor.transpose(ps_par[:, P:P + B_END], rows_b[:, :],
                                const[0:B_END, C_ID:C_ID + B_END]).then_inc(par_ps, 1)
            for u in (6, 7):
                ada_sum(b, pe, u, acc, g.acc_free, ps_mod, const[:, C_ONE:C_ONE + 1])
            for j in range(2 * KC):
                c, half = j // 2, j % 2
                if j >= 4:
                    pe.wait_ge(h32_act if half else h32_dve, c - 1)
                for i in range(4):
                    t = 4 * half + i
                    pe.wait_ge(xn_ready, TT)
                    last = nc.tensor.transpose(ps_x[:, j % 4, i * P:(i + 1) * P], x[:, t, c * P:(c + 1) * P],
                                               const[:, C_ID:C_ID + P])
                last.then_inc(xt_ps, 1)


def stage_qkv(b, g):
    nc, d = b.nc, b.dram
    n_qk = 2 * QK_CHUNKS
    n_heads = 2 * n_qk
    n_v = GROUPS * TT
    with ExitStack() as ctx:
        pos_in, folded, trig = b.sem("pos_in"), b.sem("folded"), b.sem("trig")
        sq_ready, sum_done, swap_in = b.sem("sq_ready"), b.sem("head_sums"), b.sem("swap_in")
        rot_read, rotated = b.sem("rot_read"), b.sem("qk_rotated")
        std_ready, inverted, rstd_hi, rstd_lo = b.sem("qk_std"), b.sem("qk_rstd"), b.sem("rstd_hi"), b.sem("rstd_lo")
        spread_ps, normalised = b.sem("spread_ps"), b.sem("qk_normalised")
        v_ps, v_read, link, mod_ready = b.sem("v_ps"), b.sem("v_read"), b.sem("qkv_link"), b.sem("mod_ready")
        rot = b.sb("rotated", [P, T], ctx=ctx)
        rstd = rot[0:ROWS, :]
        r_split = b.sb("rstd_split", [2 * ROWS, T], F32R, ctx)
        head_rows = b.sb("head_rows", [2 * ROWS, n_heads, HD], F32R, ctx)
        spare = g.v[:, :, :, :].rearrange("p g t n -> p (g t n)").rearrange("p (s n) -> p s n", n=T)
        cos, sin, square, turns, raw_qk = (spare[:, 0, :], spare[:, 1, :], spare[:, 2, :], spare[:, 3, :],
                                           spare[:, 4:6, :])
        angle, swapped = rot, turns
        pos = g.attn_t[:, 0, :].bitcast(I32)
        ps_a = b.ps("ps_proj", [P, 4, HALF], ctx)
        ps_s = b.ps("ps_headsums", [P, 2, HALF], ctx)
        ps_r = b.ps("ps_spread", [P, HALF], ctx)
        ps_mod = b.ps("ps_mod1", [P, HALF], ctx)
        const, par_a, mod, cact, acc = g.const, g.par_a, g.mod, g.cact, g.acc
        proj_out = lambda j: ps_a[:, 2 * (j % 2):2 * (j % 2) + 2, :].rearrange("p a n -> p (a n)")
        spread = [ps_r[:, :], ps_s[:, 0, :], ps_s[:, 1, :]]
        lag = 6
        item = lambda j: b.items[("qk", j // 2)] + j % 2
        place = g.qk
        halves = [slice(0, HALF), slice(HALF, T)]
        block = ctx.enter_context(nc.Block())

        @block.sync
        def _(sp):
            sp.dma_start(pos[:, :], d["positions"].to_broadcast([P, T])).then_inc(pos_in, 16)
            b.fetch_until(sp, "v", 2)
            b.fetch_until(sp, "ada", 23)

        @block.scalar
        def _(act):
            for at in (0, ROWS):
                nc.scalar.activation(head_rows[at:at + ROWS, :, :],
                                     const[at:at + ROWS, C_ID + at:C_ID + at + n_heads].unsqueeze(2).to_broadcast(
                                         [ROWS, n_heads, HD]), ACT.Copy).then_inc(rstd_hi, 1)
            act.wait_ge(folded, 1)
            nc.scalar.activation(sin[:, :], angle[:, :], ACT.Sin, scale=const[:, C_SIGN:C_SIGN + 1]).then_inc(trig, 1)
            nc.scalar.activation(cos[:, :], angle[:, :], ACT.Abs).then_inc(trig, 1)
            act.wait_ge(trig, 2)
            nc.scalar.activation(cos[:, :], cos[:, :], ACT.Sin, scale=-1.0,
                                 bias=const[:, C_PI2:C_PI2 + 1]).then_inc(trig, 1)
            for j in range(n_qk):
                act.wait_ge(b.pair_done, item(j) + 1)
                if j >= 1:
                    act.wait_ge(sum_done, j)
                if j >= 2:
                    act.wait_ge(rotated, j - 1)
                w = (A_QN if j < QK_CHUNKS else A_KN) + j % QK_CHUNKS
                nc.scalar.activation(square[:, :], proj_out(j), ACT.Square).then_inc(sq_ready, 1)
                nc.scalar.activation(raw_qk[:, j % 2, :], proj_out(j), ACT.Identity,
                                     scale=par_a[:, w:w + 1]).then_inc(sq_ready, 1)
                if j + 2 < n_qk:
                    b.split_high(act, "qk", (j + 2) // 2, j % 2)
                else:
                    b.split_high(act, "v", 0, j % 2)
                act.wait_ge(sq_ready, 2 * j + 2)
                if j:
                    act.wait_ge(rot_read, j)
                for n in range(4):
                    dst, src = slice(32 * n, 32 * n + 32), slice(32 * (n ^ 1), 32 * (n ^ 1) + 32)
                    act.dma_start(swapped[dst, :], raw_qk[src, j % 2, :]).then_inc(swap_in, 16)
            act.wait_ge(rotated, n_qk)
            act.wait_ge(sum_done, n_qk)
            nc.scalar.activation(rstd[:, :], ps_s[0:ROWS, :, :].rearrange("p a n -> p (a n)"), ACT.Sqrt,
                                 bias=const[0:ROWS, C_EPS:C_EPS + 1]).then_inc(std_ready, 1)
            act.wait_ge(rotated, n_qk)
            for at in range(n_v):
                act.wait_ge(v_ps, at + 1)
                nc.scalar.activation(g.v[:, at // TT, at % TT, :], ps_a[:, at % 4, 0:UNIT], ACT.Copy).then_inc(v_read, 1)
                if at == lag - 4:
                    act.wait_ge(inverted, 1)
                    nc.scalar.activation(r_split[0:ROWS, :], rstd[:, :], ACT.Copy).then_inc(rstd_hi, 1)
                if at % TT == TT - 1 and at < n_v - 1:
                    for i in range(2):
                        b.split_high(act, "v", at // TT + 1, i)

        @block.vector
        def _(dve):
            chain = Chain(dve, link)
            two_pi = 2 * np.pi
            c1 = 6.28125
            c2 = float(np.round((two_pi - c1) * 2 ** 21) / 2 ** 21)
            c3 = two_pi - c1 - c2
            magic = 1.5 * 2 ** 23
            dve.wait_ge(pos_in, 16)
            chain(nc.vector.tensor_copy(angle[:, :], pos[:, :]))
            chain(nc.vector.tensor_scalar(angle[:, :], angle[:, :], const[:, C_FREQ:C_FREQ + 1], None, ALU.mult))
            chain(nc.vector.tensor_scalar(turns[:, :], angle[:, :], 1 / two_pi, magic, ALU.mult, ALU.add))
            chain(nc.vector.tensor_scalar(turns[:, :], turns[:, :], magic, None, ALU.subtract))
            for part in (c1, c2, c3):
                chain(nc.vector.scalar_tensor_tensor(out=angle[:, :], in0=turns[:, :], scalar=-part,
                                                     in1=angle[:, :], op0=ALU.mult, op1=ALU.add))
            bound = float(np.nextafter(np.float32(np.pi), np.float32(0)))
            nc.vector.tensor_scalar(angle[:, :], angle[:, :], bound, -bound, ALU.min,
                                    ALU.max).then_inc(folded, 1)
            dve.wait_ge(trig, 3)

            def rotate(j):
                raw = raw_qk[:, j % 2, :]
                if j:
                    dve.wait_ge(rotated, j)
                dve.wait_ge(swap_in, 64 * (j + 1))
                nc.vector.tensor_tensor(rot[:, :], swapped[:, :], sin[:, :], ALU.mult).then_inc(rot_read, 1)
                chain(nc.vector.tensor_tensor(raw, raw, cos[:, :], ALU.mult))
                dve.wait_ge(rot_read, j + 1)
                nc.vector.tensor_tensor(place(j), rot[:, :], raw, ALU.add).then_inc(rotated, 1)

            for j in range(n_qk):
                if j >= 1:
                    rotate(j - 1)
                ada_unit(b, dve, chain, 8 + j, acc, g.acc_free, cact)
                if j + 2 < n_qk:
                    b.split_low(dve, "qk", (j + 2) // 2, j % 2)
                else:
                    b.split_low(dve, "v", 0, j % 2)
            rotate(n_qk - 1)
            dve.wait_ge(std_ready, 1)
            nc.vector.reciprocal(rstd[:, :], rstd[:, :]).then_inc(inverted, 1)
            dve.wait_ge(rstd_hi, 3)
            nc.vector.tensor_tensor(r_split[ROWS:2 * ROWS, :], rstd[:, :], r_split[0:ROWS, :].bitcast(F32), ALU.subtract).then_inc(rstd_lo, 1)
            dve.wait_ge(rotated, n_qk)
            for at in range(n_v + lag):
                m = at - lag
                if m >= 0:
                    j, h = divmod(m, 2)
                    dve.wait_ge(spread_ps, m + 1)
                    qk = place(j)[:, halves[h]]
                    nc.vector.tensor_tensor(qk, qk, spread[m % 3], ALU.mult).then_inc(normalised, 1)
                if at in (TT - 1, 2 * TT - 1):
                    n = at // TT
                    for i in range(2):
                        b.split_low(dve, "v", n + 1, i)
                    ada_unit(b, dve, chain, 20 + n, acc, g.acc_free, cact)
                elif at in (2 * TT + 2, 2 * TT + 4):
                    ada_unit(b, dve, chain, 22 + (at - 2 * TT - 2) // 2, acc, g.acc_free, cact)
            dve.wait_ge(g.acc_free, 24)
            chain(nc.vector.tensor_tensor(mod[:, 16:48], ps_mod[:, 16:48], par_a[:, A_BADA + 16:A_BADA + 48],
                                          ALU.add))
            nc.vector.scalar_tensor_tensor(out=mod[:, 32:40], in0=mod[:, 32:40], scalar=1.0,
                                           in1=par_a[:, A_N2:A_N2 + 8], op0=ALU.add,
                                           op1=ALU.mult).then_inc(mod_ready, 1)

        @block.tensor
        def _(pe):
            def head_sums(j):
                pe.wait_ge(sq_ready, 2 * j + 1)
                at = C_SEL + ROWS - 2 - 2 * j
                for h in range(2):
                    last = nc.tensor.matmul(ps_s[0:ROWS, h, :], const[:, at:at + ROWS], square[:, halves[h]],
                                            start=(j == 0), stop=(j == n_qk - 1))
                last.then_inc(sum_done, 1)

            b.project(proj_out(0), "qk", 0, 0, g.h_hi, g.h_lo)
            for j in range(n_qk):
                if j + 1 < n_qk:
                    if j:
                        pe.wait_ge(sq_ready, 2 * j)
                    b.project(proj_out(j + 1), "qk", (j + 1) // 2, (j + 1) % 2, g.h_hi, g.h_lo)
                head_sums(j)
                ada_sum(b, pe, 8 + j, acc, g.acc_free, ps_mod, const[:, C_ONE:C_ONE + 1])

            def spread_one(m):
                j, h = divmod(m, 2)
                if m == 0:
                    pe.wait_ge(rstd_lo, 1)
                if m >= 3:
                    pe.wait_ge(normalised, m - 2)
                two = head_rows[:, 2 * j:2 * j + 2, :].rearrange("p h n -> p (h n)")
                nc.tensor.matmul(spread[m % 3], two, r_split[:, halves[h]], start=True, stop=True).then_inc(spread_ps, 1)

            for at in range(n_v):
                n, t = divmod(at, TT)
                k = b.items[("v", n)]
                pe.wait_ge(b.split_ready, k + 2)
                if at >= 4:
                    pe.wait_ge(v_read, at - 3)
                for c in range(KC):
                    def tok(h):
                        if n == 0:
                            return h[:, c, t * P:(t + 1) * P]
                        by_class = h[:, c, :].rearrange("p (j r) -> p r j", r=4)
                        return by_class[:, t // 2, (t % 2) * P:(t % 2 + 1) * P]
                    w = lambda ring: b.shaped(ring, "v", (k + c // 4) % 2)[:, c % 4, :]
                    for m, (a, r) in enumerate(((g.h_hi, b.hi), (g.h_lo, b.hi), (g.h_hi, b.lo))):
                        last = nc.tensor.matmul(ps_a[:, at % 4, 0:UNIT], tok(a), w(r),
                                                start=(c == 0 and m == 0), stop=(c == KC - 1 and m == 2))
                    if t == TT - 1 and c == KC // 2 - 1:
                        last.then_inc(b.pair_done, 1)
                last.then_inc(v_ps, 1)
                if t == TT - 1:
                    pe.wait_ge(v_ps, at + 1)
                    pe.sem_inc(b.pair_done, 1)
                if at >= lag:
                    spread_one(at - lag)
                if at in (TT + 2, 2 * TT + 2):
                    ada_sum(b, pe, 20 + at // TT - 1, acc, g.acc_free, ps_mod, const[:, C_ONE:C_ONE + 1])
            for m in range(n_v - lag, n_v):
                spread_one(m)
            for u in (22, 23):
                ada_sum(b, pe, u, acc, g.acc_free, ps_mod, const[:, C_ONE:C_ONE + 1])


def stage_attention(b, g):
    nc = b.nc
    units = [(c, i, s) for c in range(4) for i in range(2) for s in range(SLOTS)]
    n_units = len(units)
    with ExitStack() as ctx:
        s_ps, s_read, max_ready, p_ready = b.sem("s_ps"), b.sem("s_read"), b.sem("max_ready"), b.sem("p_ready")
        t_ps, t_read_act, t_read_dve = b.sem("t_ps"), b.sem("t_read_act"), b.sem("t_read_dve")
        pv_done, o_read, link = b.sem("pv_done"), b.sem("o_read"), b.sem("attn_link")
        prob = b.sb("prob", [P, 2, KEYS], ctx=ctx)
        prob_t = b.sb("prob_t", [P, KEYS], ctx=ctx)
        stat = b.sb("stat", [P, 4, 6], ctx=ctx)
        attn = g.acc
        ps_s = b.ps("ps_s", [P, 3, HALF], ctx)
        ps_t = b.ps("ps_t", [P, 3, HALF], ctx)
        ps_o = b.ps("ps_o", [P, 2, HALF], ctx)
        const = g.const
        flat_s = ps_s[:, :, :].rearrange("p a n -> p (a n)")
        flat_t = ps_t[:, :, :].rearrange("p a n -> p (a n)")
        ident = const[:, C_ID:C_ID + P]
        block = ctx.enter_context(nc.Block())

        def classes(ap):
            return ap.rearrange("p (j r) -> p r j", r=4)

        def heads(first, group, s):
            base = HD * (s % 2)
            return g.qk(first + 2 * group + s // 2)[base:base + HD, :]

        @block.tensor
        def _(pe):
            def scores(u):
                c, i, s = units[u]
                if u:
                    pe.wait_ge(s_read, u)
                for group in range(GROUPS):
                    q = classes(heads(0, group, s))[:, c, i * P:(i + 1) * P]
                    k = heads(QK_CHUNKS, group, s)
                    if group == 0:
                        at = 384 * i
                        parts = [(0, k[:, at:at + HALF]), (HALF, k[:, at + HALF:at + G0_KEYS])]
                    else:
                        parts = [((G0_KEYS, 2 * HALF)[group - 1], classes(k)[:, c, :])]
                    for col, keys in parts:
                        last = nc.tensor.matmul(flat_s[:, col:col + keys.shape[1]], q, keys, start=True, stop=True)
                last.then_inc(s_ps, 1)

            def transpose(u):
                pe.wait_ge(p_ready, u + 1)
                if u:
                    pe.wait_ge(t_read_act, u)
                    pe.wait_ge(t_read_dve, u)
                if u >= 5 and u % 4 == 1:
                    attn_out(u // 4 - 1)
                for n in range(KEYS // P):
                    last = nc.tensor.transpose(flat_t[:, n * P:(n + 1) * P], prob[:, u % 2, n * P:(n + 1) * P], ident)
                last.then_inc(t_ps, 1)

            def attn_out(tile):
                pe.wait_ge(o_read, SLOTS * (tile + 1))
                for ch in range(2):
                    last = nc.tensor.transpose(ps_t[:, 2, (1 + ch) * P:(2 + ch) * P],
                                               attn[:, tile % 2, ch * P:(ch + 1) * P], ident)
                return last

            def values(u):
                c, i, s = units[u]
                pe.wait_ge(t_read_act, u + 1)
                pe.wait_ge(t_read_dve, u + 1)
                if u >= 2:
                    pe.wait_ge(o_read, u - 1)
                tiles = [(0, 3 * i + n) for n in range(5)] + [(1, 2 * c), (1, 2 * c + 1), (2, 2 * c), (2, 2 * c + 1)]
                for n, (group, t) in enumerate(tiles):
                    last = nc.tensor.matmul(ps_o[:, u % 2, 0:HD], prob_t[:, n * P:(n + 1) * P],
                                            g.v[:, group, t, s * HD:(s + 1) * HD],
                                            start=(n == 0), stop=(n == len(tiles) - 1))
                last.then_inc(pv_done, 1)

            for step in range(n_units + 2):
                if step < n_units:
                    scores(step)
                if 1 <= step <= n_units:
                    transpose(step - 1)
                if step >= 2:
                    values(step - 2)
            pe.wait_ge(t_read_dve, n_units)
            attn_out(7).then_inc(t_ps, 1)

        @block.scalar
        def _(act):
            def evacuate(u):
                act.wait_ge(t_ps, u + 1)
                if u:
                    act.wait_ge(pv_done, u)
                nc.scalar.activation(prob_t[:, 0:HALF], ps_t[:, 0, :], ACT.Copy).then_inc(t_read_act, 1)

            for i in range(2):
                b.split_high(act, "xy", 0, i)
            for u in range(n_units):
                act.wait_ge(max_ready, u + 1)
                nc.scalar.activation(prob[:, u % 2, :], prob[:, u % 2, :], ACT.Exp, bias=stat[:, u % 4, 3:4],
                                     accum_out=stat[:, u % 4, 4:5]).then_inc(p_ready, 1)
                if u:
                    evacuate(u - 1)
            evacuate(n_units - 1)

        @block.vector
        def _(dve):
            chain = Chain(dve, link)

            def maximum(u):
                c, i, s = units[u]
                st = stat[:, u % 4, :]
                if u >= 2:
                    dve.wait_ge(t_ps, u - 1)
                dve.wait_ge(s_ps, u + 1)
                m0, m1 = C_M0 + M0_PAD - c - P * i, C_M1 + P - P * i
                parts = [(0, 0, G0_KEYS, m0), (G0_KEYS, G0_KEYS, G12_KEYS, m1),
                         (G0_KEYS + G12_KEYS, 2 * HALF, G12_KEYS, C_M2)]
                for n, (dst, src, width, mask) in enumerate(parts):
                    ins = nc.vector.tensor_tensor_reduce(
                        out=prob[:, u % 2, dst:dst + width], in0=flat_s[:, src:src + width],
                        in1=const[:, mask:mask + width], scale=HD ** -0.5,
                        scalar=st[:, n - 1:n] if n else -3e38, op0=ALU.add, op1=ALU.max,
                        accum_out=st[:, n:n + 1])
                    if n < 2:
                        chain(ins)
                ins.then_inc(s_read, 1)
                dve.wait_ge(s_read, u + 1)
                nc.vector.tensor_scalar(st[:, 3:4], st[:, 2:3], -1.0, None, ALU.mult).then_inc(max_ready, 1)

            def attn_evacuate(tile):
                c, i = divmod(tile, 2)
                out = g.attn_t[:, :, :].rearrange("p a (j r) -> p a r j", r=4)[:, :, c, i * P:(i + 1) * P]
                return nc.vector.tensor_copy(out, ps_t[:, 2, P:3 * P].rearrange("p (a n) -> p a n", a=2))

            def evacuate(u):
                dve.wait_ge(t_ps, u + 1)
                if u:
                    dve.wait_ge(pv_done, u)
                if u >= 5 and u % 4 == 1:
                    attn_evacuate(u // 4 - 1)
                nc.vector.tensor_copy(prob_t[:, HALF:KEYS], flat_t[:, HALF:KEYS]).then_inc(t_read_dve, 1)

            def normalise(u):
                tile, s = divmod(u, SLOTS)
                st = stat[:, u % 4, :]
                dve.wait_ge(pv_done, u + 1)
                chain(nc.vector.reciprocal(st[:, 5:6], st[:, 4:5]))
                nc.vector.tensor_scalar(attn[:, tile % 2, s * HD:(s + 1) * HD], ps_o[:, u % 2, 0:HD],
                                        st[:, 5:6], None, ALU.mult).then_inc(o_read, 1)

            for i in range(2):
                b.split_low(dve, "xy", 0, i)
            for step in range(n_units + 2):
                if step < n_units:
                    maximum(step)
                if 1 <= step <= n_units:
                    evacuate(step - 1)
                if step >= 2:
                    normalise(step - 2)
            dve.wait_ge(t_ps, n_units + 1)
            attn_evacuate(7).then_inc(t_read_dve, 1)


def stage_lru(b, g):
    nc, d = b.nc, b.dram
    with ExitStack() as ctx:
        names = ["gate_in", "wg_hi", "wg_lo", "zeroed", "conv_done", "xc_hi", "xc_lo", "gates_f", "gates_b",
                 "tanh_f", "tanh_b", "a2_f", "a2_b", "z_f", "z_b", "ix_f", "ix_b", "sqrt_f", "sqrt_b", "u_f", "u_b",
                 "scan_f", "lru_done", "gelu_done", "lam_exp", "decay"]
        sem = {n: b.sem("lru_" + n) for n in names}
        link_dve, link_act = b.sem("lru_link_dve"), b.sem("lru_link_act")
        wg = g.acc[:, :, :].rearrange("p a (w n) -> p (a w) n", n=P)
        wg_hi, wg_lo = b.sb("wg_hi", [P, 4, P], F32R, ctx), b.sb("wg_lo", [P, 4, P], F32R, ctx)
        recur, inp, decay, root, xc = (g.area[:, 2 * n * T:2 * (n + 1) * T].rearrange("p (a n) -> p a n", a=2)
                                       for n in range(5))
        xc_hi, xc_lo = b.sb("xc_hi", [P, T], F32R, ctx), b.sb("xc_lo", [P, T], F32R, ctx)
        small = b.sb("small", [P, 4, 16], ctx=ctx)
        c4, c4n, half_bias = b.sb("c4", [P, 16], ctx=ctx), b.sb("c4n", [P, 16], ctx=ctx), b.sb("hb", [P, 32], ctx=ctx)
        ps_x, ps_y = g.ps_proj[:, 0:2, :], g.ps_proj[:, 2:4, :]
        ps_ga, ps_gx = b.ps("ps_gate_a", [P, 2, HALF], ctx), b.ps("ps_gate_x", [P, 2, HALF], ctx)
        flat = lambda t: t[:, :, :].rearrange("p a n -> p (a n)")
        par = g.par_b
        col = lambda at: par[:, at:at + 1]
        item = lambda j, i: b.items[("xy", j)] + i
        F, B = 0, 1
        block = ctx.enter_context(nc.Block())

        @block.sync
        def _(sp):
            b.fetch_until(sp, "xy", KC - 1)

        @block.gpsimd
        def _(pool):
            nc.gpsimd.memset(wg[:, :, :], 0.0).then_inc(sem["zeroed"], 1)
            pool.wait_ge(sem["zeroed"], 1)
            for j in range(KC):
                if j:
                    pool.wait_ge(sem["wg_lo"], j)
                for w, name in enumerate(("lru_w_a", "lru_w_x")):
                    for h in range(2):
                        dst = wg[HD * h:HD * (h + 1), w::2, HD * h:HD * (h + 1)]
                        src = d[name][0, :, 2 * j + h].rearrange("w k n -> k w n")
                        pool.dma_start(dst, src).then_inc(sem["gate_in"], 16)

        @block.scalar
        def _(act):
            link = Chain(act, link_act)

            def gate_weights(j):
                act.wait_ge(sem["gate_in"], 64 * (j + 1))
                if j:
                    act.wait_ge(sem["gates_b"], j)
                nc.scalar.activation(wg_hi[:, :, :], wg[:, :, :], ACT.Copy).then_inc(sem["wg_hi"], 1)

            def conv_high(j):
                act.wait_ge(sem["conv_done"], j + 1)
                if j:
                    act.wait_ge(sem["gates_b"], j)
                nc.scalar.activation(xc_hi[:, :], xc[:, j % 2, :], ACT.Copy).then_inc(sem["xc_hi"], 1)

            def gelu(j):
                act.wait_ge(b.pair_done, item(j, 1) + 1)
                nc.scalar.activation(g.lru_t[:, j, :], flat(ps_y), ACT.Gelu_apprx_tanh).then_inc(sem["gelu_done"], 1)

            def direction(j, way, gates, tanh, z_done, u_done, last_read, a2_done):
                k = KC * way + j
                act.wait_ge(sem[gates], j + 1)
                if j:
                    act.wait_ge(sem[z_done], j)
                nc.scalar.activation(recur[:, way, :], flat(ps_ga), ACT.Tanh, scale=0.5,
                                     bias=half_bias[:, k:k + 1]).then_inc(sem[tanh], 1)
                if j:
                    act.wait_ge(sem[last_read], j)
                nc.scalar.activation(inp[:, way, :], flat(ps_gx), ACT.Tanh, scale=0.5,
                                     bias=half_bias[:, 16 + k:17 + k]).then_inc(sem[tanh], 1)
                act.wait_ge(sem[tanh], 2 * j + 1)
                link(nc.scalar.activation(decay[:, way, :], recur[:, way, :], ACT.Exp, scale=c4[:, k:k + 1],
                                          bias=c4[:, k:k + 1]))
                link(nc.scalar.activation(root[:, way, :], recur[:, way, :], ACT.Tanh, scale=c4n[:, k:k + 1],
                                          bias=c4n[:, k:k + 1]))
                nc.scalar.activation(recur[:, way, :], decay[:, way, :], ACT.Square).then_inc(sem[a2_done], 1)

            link(nc.scalar.activation(small[:, 0, :], par[:, B_LAM:B_LAM + 16], ACT.Abs))
            nc.scalar.activation(small[:, 0, :], small[:, 0, :], ACT.Exp, scale=-1.0).then_inc(sem["lam_exp"], 1)
            gate_weights(0)
            for i in range(2):
                b.split_high(act, "xy", 1, i)
            conv_high(0)
            gelu(0)
            act.wait_ge(sem["decay"], 1)
            def next_item(j, i):
                if j + 2 < KC:
                    b.split_high(act, "xy", j + 2, i)
                elif j + 2 == KC:
                    b.split_high(act, "ga", 0, i)

            for j in range(KC):
                next_item(j, 0)
                direction(j, F, "gates_f", "tanh_f", "z_f", "u_f", "scan_f", "a2_f")
                next_item(j, 1)
                direction(j, B, "gates_b", "tanh_b", "z_b", "u_b", "lru_done", "a2_b")
                if j + 1 < KC:
                    gate_weights(j + 1)
                    conv_high(j + 1)
                for way, z, done in ((F, "z_f", "sqrt_f"), (B, "z_b", "sqrt_b")):
                    act.wait_ge(sem[z], j + 1)
                    nc.scalar.activation(root[:, way, :], root[:, way, :], ACT.Sqrt).then_inc(sem[done], 1)
                if j + 1 < KC:
                    gelu(j + 1)

        @block.vector
        def _(dve):
            link = Chain(dve, link_dve)

            def conv(j):
                dve.wait_ge(b.pair_done, item(j, 0) + 1)
                if j >= 2:
                    dve.wait_ge(sem["lru_done"], j - 1)
                y, x = xc[:, j % 2, :], flat(ps_x)
                w = lambda tap: col(B_CW + KC * tap + j)
                link(nc.vector.tensor_scalar(y, x, w(2), col(B_CB + j), ALU.mult, ALU.add))
                for tap, dst, src in ((0, y[:, 2:T], x[:, 0:T - 2]), (1, y[:, 1:T], x[:, 0:T - 1]),
                                      (3, y[:, 0:T - 1], x[:, 1:T])):
                    ins = nc.vector.scalar_tensor_tensor(out=dst, in0=src, scalar=w(tap), in1=dst,
                                                         op0=ALU.mult, op1=ALU.add)
                    if tap < 3:
                        link(ins)
                ins.then_inc(sem["conv_done"], 1)

            def lows(j):
                dve.wait_ge(sem["wg_hi"], j + 1)
                nc.vector.tensor_tensor(wg_lo[:, :, :], wg[:, :, :], wg_hi[:, :, :].bitcast(F32),
                                        ALU.subtract).then_inc(sem["wg_lo"], 1)
                dve.wait_ge(sem["xc_hi"], j + 1)
                nc.vector.tensor_tensor(xc_lo[:, :], xc[:, j % 2, :], xc_hi[:, :].bitcast(F32),
                                        ALU.subtract).then_inc(sem["xc_lo"], 1)

            def before_root(j, way, a2, z, tanh, ix):
                dve.wait_ge(sem[a2], j + 1)
                nc.vector.scalar_tensor_tensor(out=root[:, way, :], in0=recur[:, way, :], scalar=1.0,
                                               in1=root[:, way, :], op0=ALU.add, op1=ALU.mult).then_inc(sem[z], 1)
                dve.wait_ge(sem[tanh], 2 * j + 2)
                nc.vector.scalar_tensor_tensor(out=inp[:, way, :], in0=inp[:, way, :], scalar=1.0,
                                               in1=xc[:, j % 2, :], op0=ALU.add, op1=ALU.mult).then_inc(sem[ix], 1)

            def after_root(j, way, root_done, ix, u):
                dve.wait_ge(sem[root_done], j + 1)
                dve.wait_ge(sem[ix], j + 1)
                nc.vector.scalar_tensor_tensor(out=inp[:, way, :], in0=inp[:, way, :], scalar=0.5,
                                               in1=root[:, way, :], op0=ALU.mult, op1=ALU.mult).then_inc(sem[u], 1)
                dve.wait_ge(sem[u], j + 1)

            e, s, s2, q = (small[:, n, :] for n in range(4))
            dve.wait_ge(sem["lam_exp"], 1)
            link(nc.vector.tensor_scalar(s, e, 2.0, None, ALU.add))
            link(nc.vector.reciprocal(s, s))
            link(nc.vector.tensor_tensor(s, e, s, ALU.mult))
            link(nc.vector.tensor_tensor(s2, s, s, ALU.mult))
            link(nc.vector.tensor_scalar(q, s2, 1.0 / 17, None, ALU.mult))
            for n in (15, 13, 11, 9, 7, 5, 3):
                link(nc.vector.scalar_tensor_tensor(out=q, in0=q, scalar=1.0 / n, in1=s2, op0=ALU.add, op1=ALU.mult))
            link(nc.vector.scalar_tensor_tensor(out=q, in0=q, scalar=1.0, in1=s, op0=ALU.add, op1=ALU.mult))
            link(nc.vector.tensor_scalar(q, q, 2.0, None, ALU.mult))
            link(nc.vector.tensor_scalar(s, par[:, B_LAM:B_LAM + 16], -1.0, 0.0, ALU.mult, ALU.max))
            link(nc.vector.tensor_tensor(q, q, s, ALU.add))
            link(nc.vector.tensor_scalar(c4[:, :], q, -4.0, None, ALU.mult))
            link(nc.vector.tensor_scalar(c4n[:, :], q, 4.0, None, ALU.mult))
            nc.vector.tensor_scalar(half_bias[:, :], par[:, B_BA:B_BA + 32], 0.5, None,
                                    ALU.mult).then_inc(sem["decay"], 1)
            conv(0)
            for i in range(2):
                b.split_low(dve, "xy", 1, i)
            lows(0)
            def next_item(j, i):
                if j + 2 < KC:
                    b.split_low(dve, "xy", j + 2, i)
                elif j + 2 == KC:
                    b.split_low(dve, "ga", 0, i)

            for j in range(KC):
                if j + 1 < KC:
                    conv(j + 1)
                next_item(j, 0)
                before_root(j, F, "a2_f", "z_f", "tanh_f", "ix_f")
                next_item(j, 1)
                before_root(j, B, "a2_b", "z_b", "tanh_b", "ix_b")
                if j + 1 < KC:
                    lows(j + 1)
                after_root(j, F, "sqrt_f", "ix_f", "u_f")
                h = xc[:, j % 2, :]
                dve.wait_ge(sem["ix_b"], j + 1)
                nc.vector.tensor_tensor_scan(h, decay[:, F, :], inp[:, F, :], 0.0, ALU.mult,
                                             ALU.add).then_inc(sem["scan_f"], 1)
                after_root(j, B, "sqrt_b", "ix_b", "u_b")
                back = inp[:, B, ::-1]
                link(nc.vector.tensor_tensor_scan(back, decay[:, B, ::-1], back, 0.0, ALU.mult, ALU.add))
                dve.wait_ge(sem["scan_f"], j + 1)
                link(nc.vector.tensor_tensor(h, h, inp[:, B, :], ALU.add))
                dve.wait_ge(sem["gelu_done"], j + 1)
                nc.vector.tensor_tensor(g.lru_t[:, j, :], g.lru_t[:, j, :], h, ALU.mult).then_inc(sem["lru_done"], 1)

        @block.tensor
        def _(pe):
            def gates(j, way, done):
                for a, out in ((0, ps_ga), (1, ps_gx)):
                    w = 2 * way + a
                    for h in range(2):
                        cols = slice(h * HALF, (h + 1) * HALF)
                        for m, (l, r) in enumerate(((wg_hi, xc_hi), (wg_hi, xc_lo), (wg_lo, xc_hi))):
                            last = nc.tensor.matmul(out[:, h, :], l[:, w, :], r[:, cols], start=(m == 0), stop=(m == 2))
                last.then_inc(sem[done], 1)

            b.project(flat(ps_x), "xy", 0, 0, g.h_hi, g.h_lo)
            b.project(flat(ps_y), "xy", 0, 1, g.h_hi, g.h_lo)
            for j in range(KC):
                kind, n = ("xy", j + 1) if j + 1 < KC else ("ga", 0)
                pe.wait_ge(sem["conv_done"], j + 1)
                b.project(flat(ps_x), kind, n, 0, g.h_hi, g.h_lo)
                pe.wait_ge(sem["wg_lo"], j + 1)
                pe.wait_ge(sem["xc_lo"], j + 1)
                if j:
                    pe.wait_ge(sem["tanh_b"], 2 * j)
                gates(j, F, "gates_f")
                if j + 1 < KC:
                    pe.wait_ge(sem["gelu_done"], j + 1)
                    b.project(flat(ps_y), kind, n, 1, g.h_hi, g.h_lo)
                pe.wait_ge(sem["tanh_f"], 2 * j + 2)
                gates(j, B, "gates_b")
            pe.wait_ge(sem["gelu_done"], KC)
            b.project(flat(ps_y), "ga", 0, 1, g.h_hi, g.h_lo)


def stage_merge(b, g):
    nc = b.nc
    with ExitStack() as ctx:
        gate_tanh, branch_ps, merged_done = b.sem("gate_tanh"), b.sem("branch_ps"), b.sem("merged_done")
        lru_gated, attn_read = b.sem("lru_branch_gated"), b.sem("attn_branch_read")
        piece_hi_ready, piece_lo_ready, piece_done = b.sem("piece_hi"), b.sem("piece_lo"), b.sem("piece_done")
        step_ps, left_act, left_dve = b.sem("lru_step_ps"), b.sem("lru_left_act"), b.sem("lru_left_dve")
        piece_hi, piece_lo = b.sb("piece_hi_ring", [P, 2, HALF], F32R, ctx), b.sb("piece_lo_ring", [P, 2, HALF], F32R, ctx)
        gate = lambda q: g.area[:, (KC + q) * T:(KC + q + 1) * T] if q < 2 else g.lru_t[:, q - 2, :]
        ps_g = g.ps_proj
        ps_b = b.ps("ps_branch", [P, 4, HALF], ctx)
        ps_a = lambda i: ps_b[:, 2 * i:2 * i + 2, :]
        flat = lambda t: t[:, :, :].rearrange("p a n -> p (a n)")
        gate_out = lambda n: ps_g[:, 2 * (n % 2):2 * (n % 2) + 2, :].rearrange("p a n -> p (a n)")
        pairs = KC // 2
        kinds = [("ga", 0), ("ga", 1), ("gl", 0), ("gl", 1)]
        item = lambda n, q: b.items[(kinds[q][0], n)] + kinds[q][1]
        steps = [(o, h) for o in range(2) for h in range(2)]
        n_pieces = len(steps) * KC
        lru_item = lambda k: b.items[("lru", k // 4)] + k % 4 // 2
        piece = lambda k: g.lru_t[:, k % KC, steps[k // KC][1] * HALF:(steps[k // KC][1] + 1) * HALF]
        block = ctx.enter_context(nc.Block())

        def piece_free(eng, k):
            if k >= 2 and k % 2 == 0:
                eng.wait_ge(piece_done, k // 2)
            elif k >= 2:
                eng.wait_ge(b.pair_done, lru_item(k - 2) + 1)

        def leave(eng, step, banks, copy):
            o, h = steps[step]
            for n in banks:
                if n < 3:
                    eng.wait_ge(step_ps, 3 * step + n + 1)
                else:
                    eng.wait_ge(b.pair_done, lru_item(KC * step + KC - 1) + 1)
                copy(g.merged[:, 4 * o + n, h * HALF:(h + 1) * HALF], ps_b[:, n, :])

        @block.sync
        def _(sp):
            b.fetch_count(sp, len(b.plan))

        @block.scalar
        def _(act):
            copy = lambda dst, src: nc.scalar.activation(dst, src, ACT.Copy).then_inc(left_act, 1)
            for k in range(n_pieces):
                if k % 2 == 0:
                    b.split_high(act, "lru", k // 4, k % 4 // 2)
                piece_free(act, k)
                nc.scalar.activation(piece_hi[:, k % 2, :], piece(k), ACT.Copy).then_inc(piece_hi_ready, 1)
                if k and k % KC == 0:
                    leave(act, k // KC - 1, (0, 1), copy)
            for i in range(2):
                b.split_high(act, "gl", 0, i)
            leave(act, len(steps) - 1, (0, 1), copy)
            for n in range(pairs):
                for q in range(4):
                    act.wait_ge(b.pair_done, item(n, q) + 1)
                    if n:
                        act.wait_ge(merged_done, 2 * n - 1 + q % 2)
                    nc.scalar.activation(gate(q), gate_out(q), ACT.Tanh, scale=0.5).then_inc(gate_tanh, 1)
                    if q < 2 and n:
                        b.split_high(act, "gl", n, q)
                    elif q >= 2 and n + 1 < pairs:
                        b.split_high(act, "ga", n + 1, q - 2)
            for n in range(2):
                out_high(b, act, g, n)

        @block.vector
        def _(dve):
            copy = lambda dst, src: nc.vector.tensor_copy(dst, src).then_inc(left_dve, 1)
            for k in range(n_pieces):
                if k % 2 == 0:
                    b.split_low(dve, "lru", k // 4, k % 4 // 2)
                dve.wait_ge(piece_hi_ready, k + 1)
                nc.vector.tensor_tensor(piece_lo[:, k % 2, :], piece(k), piece_hi[:, k % 2, :].bitcast(F32),
                                        ALU.subtract).then_inc(piece_lo_ready, 1)
                if k and k % KC == 0:
                    leave(dve, k // KC - 1, (2, 3), copy)
            for i in range(2):
                b.split_low(dve, "gl", 0, i)
            leave(dve, len(steps) - 1, (2, 3), copy)
            dve.wait_ge(left_act, 2 * len(steps))
            dve.wait_ge(left_dve, 2 * len(steps))
            for n in range(pairs):
                for q in range(4):
                    if q < 2 and n:
                        b.split_low(dve, "gl", n, q)
                    elif q >= 2 and n + 1 < pairs:
                        b.split_low(dve, "ga", n + 1, q - 2)
                if n == pairs - 1:
                    for m in range(2):
                        out_low(b, dve, g, m)
                for i in range(2):
                    c = 2 * n + i
                    dve.wait_ge(gate_tanh, 4 * n + 3 + i)
                    nc.vector.scalar_tensor_tensor(out=gate(2 + i), in0=gate(2 + i), scalar=1.0, in1=g.merged[:, c, :],
                                                   op0=ALU.add, op1=ALU.mult).then_inc(lru_gated, 1)
                    dve.wait_ge(branch_ps, c + 1)
                    nc.vector.scalar_tensor_tensor(out=gate(i), in0=gate(i), scalar=1.0, in1=flat(ps_a(i)),
                                                   op0=ALU.add, op1=ALU.mult).then_inc(attn_read, 1)
                    dve.wait_ge(lru_gated, c + 1)
                    dve.wait_ge(attn_read, c + 1)
                    nc.vector.tensor_tensor(g.merged[:, c, :], gate(i), gate(2 + i), ALU.add).then_inc(merged_done, 1)

        @block.tensor
        def _(pe):
            for k in range(n_pieces):
                step, c = divmod(k, KC)
                if k % 2 == 0:
                    pe.wait_ge(b.split_ready, lru_item(k) + 1)
                pe.wait_ge(piece_lo_ready, k + 1)
                whi, wlo = (b.shaped(r, "lru", lru_item(k) % 2)[:, c % 2, :] for r in (b.hi, b.lo))
                for n in range(4):
                    if c == 0 and step:
                        pe.wait_ge(left_act if n < 2 else left_dve, 2 * step - 1 + n % 2)
                    cols = slice(n * P, (n + 1) * P)
                    for m, (w, a) in enumerate(((whi, piece_hi), (whi, piece_lo), (wlo, piece_hi))):
                        last = nc.tensor.matmul(ps_b[:, n, :], w[:, cols], a[:, k % 2, :],
                                                start=(c == 0 and m == 0), stop=(c == KC - 1 and m == 2))
                    if c == KC - 1 and n < 3:
                        last.then_inc(step_ps, 1)
                last.then_inc(piece_done if k % 2 == 0 else b.pair_done, 1)
            for n in range(pairs):
                for q, (kind, i) in enumerate(kinds):
                    if 4 * n + q < 2:
                        continue
                    pe.wait_ge(gate_tanh, 4 * n + q - 1)
                    b.project(gate_out(q), kind, n, i, g.h_hi, g.h_lo)
                w_attn = b.unit("attn", n)
                b.arrived(pe, "attn", n)
                if n == 0:
                    pe.wait_ge(left_act, 2 * len(steps))
                    pe.wait_ge(left_dve, 2 * len(steps))
                for i in range(2):
                    if n:
                        pe.wait_ge(attn_read, 2 * n + i - 1)
                    for h in range(2):
                        for c in range(2):
                            last = nc.tensor.matmul(ps_a(i)[:, h, :], w_attn[:, c, i * P:(i + 1) * P],
                                                    g.attn_t[:, c, h * HALF:(h + 1) * HALF],
                                                    start=(c == 0), stop=(c == 1))
                    last.then_inc(branch_ps, 1)
                pe.wait_ge(branch_ps, 2 * n + 2)
                pe.sem_inc(b.raw_pe, 1)


def stage_out(b, g, out, h2_dram):
    nc, d = b.nc, b.dram
    with ExitStack() as ctx:
        names = ["router_in", "x_in0", "x_in1", "rows_ps", "rows_ready", "m_hi", "m_lo", "mix_ps",
                 "x1_ready", "square", "std", "h2_ready", "tr_ps", "tr_read", "logit_ps", "logits", "shifted",
                 "exped", "affinity", "aff_ps", "aff_ready", "chosen", "choice_ps", "stored_x1_0", "stored_x1_1", "stored_h2_0", "stored_h2_1"]
        sem = {n: b.sem("out_" + n) for n in names}
        link = b.sem("out_link")
        w_hi, w_lo = g.h_hi, g.h_lo
        tile_hi, tile_lo = split_rings(g)
        spare = g.lru_t
        rows = lambda r: spare[:, r, :] if r < 2 else g.attn_t[:, 0, :]
        h2_t = g.attn_t[:, 1, :].rearrange("p (c n) -> p c n", n=P)
        x, x1, h2 = spare[:, 2:4, :], spare[:, 4:6, :], spare[:, 6:8, :]
        m_hi, m_lo = (ring[:, :, :].rearrange("p a (c n) -> p a c n", n=P) for ring in (b.hi, b.lo))
        router = b.sb("router", [P, KC, E], ctx=ctx)
        stat = b.sb("out_stat", [P, 2, 3], ctx=ctx)
        logits, soft = b.sb("logits", [P, 4, 2, E], ctx=ctx), b.sb("soft", [P, 3, TT], ctx=ctx)
        ps_mix = b.ps("ps_mix", [P, 4, HALF], ctx)
        ps_tr, ps_log, ps_choice = b.ps("ps_tr", [P, 2, HALF], ctx), b.ps("ps_log", [P, HALF], ctx), b.ps("ps_choice", [P, HALF], ctx)
        const, mod = g.const, g.mod
        logits_flat = logits[:, :, :, :].rearrange("p a b e -> p (a b e)")
        by_tile = logits[:, :, :, :].rearrange("p a b e -> p (a b) e")
        ident = const[:, C_ID:C_ID + P]
        flat_tr = ps_tr[:, :, :].rearrange("p a n -> p (a n)")
        mix = lambda t: ps_mix[:, 2 * (t % 2):2 * (t % 2) + 2, :].rearrange("p a n -> p (a n)")
        aff = h2_t[0:2 * E, 0:4, :].rearrange("p c n -> p (c n)")
        best_at = b.sb("best_at", [2 * E, CAP], U32, ctx)
        lists = b.sb("best_lists", [2 * E, 4, CAP], ctx=ctx)
        best, best_at_f, best_up, best_at_up = (lists[:, n, :] for n in range(4))
        pick = b.sb("pick", [P, 2, E], ctx=ctx)
        x_dram = d["x"][0]
        block = ctx.enter_context(nc.Block())
        row_cols = [16, 32, 24]
        row_banks = lambda r: (ps_log[:, :], ps_choice[:, :]) if r == 1 else (ps_tr[:, 0, :], ps_tr[:, 1, :])

        @block.sync
        def _(sp):
            sp.dma_start(router[:, :, :], d["w_router"][0].rearrange("(c p) n -> p c n", p=P)
                         ).then_inc(sem["router_in"], 16)
            for t in range(2):
                sp.dma_start(x[:, t, :], x_dram[t * P:(t + 1) * P, :]).then_inc(sem[f"x_in{t}"], 16)
            for t in range(TT):
                if t == TT - 1:
                    sp.wait_ge(b.out_read, 4)
                    sp.wait_ge(sem["m_hi"], TT)
                    sp.wait_ge(sem["m_lo"], TT)
                    for n in range(EARLY_TILES):
                        fetch_tile(d, g, sp, 0, n)
                sp.wait_ge(sem["x1_ready"], t + 1)
                sp.dma_start(out[0, t * P:(t + 1) * P, :], x1[:, t % 2, :]).then_inc(sem[f"stored_x1_{t % 2}"], 16)
                if t + 2 < TT:
                    sp.dma_start(x[:, t % 2, :], x_dram[(t + 2) * P:(t + 3) * P, :]).then_inc(sem[f"x_in{t % 2}"], 16)
                sp.wait_ge(sem["h2_ready"], t + 1)
                sp.dma_start(h2_dram[t * P:(t + 1) * P, :], h2[:, t % 2, :]).then_inc(sem[f"stored_h2_{t % 2}"], 16)
            for t in range(2):
                sp.wait_ge(sem[f"stored_x1_{t}"], 8 * TT)
                sp.wait_ge(sem[f"stored_h2_{t}"], 8 * TT)

        @block.scalar
        def _(act):
            def row(r):
                act.wait_ge(sem["rows_ps"], r + 1)
                for h, bank in enumerate(row_banks(r)):
                    nc.scalar.activation(rows(r)[:, h * HALF:(h + 1) * HALF], bank, ACT.Copy,
                                         scale=0.5 if r == 0 else 1.0).then_inc(sem["rows_ready"], 1)

            def m_high(t):
                if t >= 2:
                    act.wait_ge(sem["mix_ps"], t - 1)
                nc.scalar.activation(m_hi[:, t % 2, :, :], g.merged[:, :, t * P:(t + 1) * P],
                                     ACT.Copy).then_inc(sem["m_hi"], 1)

            m_high(0)
            out_high(b, act, g, 2)
            row(0)
            out_high(b, act, g, 3)
            row(1)
            m_high(1)
            row(2)
            for t in range(TT):
                act.wait_ge(sem["x1_ready"], t + 1)
                if t >= 2:
                    act.wait_ge(sem[f"stored_h2_{t % 2}"], 16 * (t // 2))
                    act.wait_ge(sem["tr_ps"], t - 1)
                nc.scalar.activation(h2[:, t % 2, :], x1[:, t % 2, :], ACT.Square,
                                     accum_out=stat[:, t % 2, 0:1]).then_inc(sem["square"], 1)
                act.wait_ge(sem["square"], t + 1)
                nc.scalar.activation(stat[:, t % 2, 1:2], stat[:, t % 2, 0:1], ACT.Sqrt, scale=1.0 / D,
                                     bias=const[:, C_EPS:C_EPS + 1]).then_inc(sem["std"], 1)
                if t + 2 < TT:
                    m_high(t + 2)
                act.wait_ge(sem["tr_ps"], t + 1)
                if t:
                    act.wait_ge(sem["logit_ps"], t)
                nc.scalar.activation(h2_t[:, :, :].rearrange("p c n -> p (c n)"), flat_tr,
                                     ACT.Copy).then_inc(sem["tr_read"], 1)
            act.wait_ge(sem["shifted"], 1)
            nc.scalar.activation(logits_flat, logits_flat, ACT.Exp).then_inc(sem["exped"], 1)
            act.wait_ge(sem["aff_ps"], 1)
            act.wait_ge(sem["logit_ps"], TT)
            nc.scalar.activation(aff, flat_tr[0:2 * E, 0:HALF], ACT.Copy).then_inc(sem["aff_ready"], 1)
            act.wait_ge(sem["mix_ps"], TT)
            for n in range(SPLIT_AHEAD):
                act.wait_ge(g.tile_in[n], 16)
                for i in range(2):
                    nc.scalar.activation(half(tile_hi[:, n, :], i), half(raw_tile(g, n), i), ACT.Copy).then_inc(g.hi_ready, 1)

        @block.gpsimd
        def _(pool):
            for n in range(SPLIT_AHEAD):
                for i in range(2):
                    pool.wait_ge(g.hi_ready, 2 * n + i + 1)
                    nc.gpsimd.tensor_tensor(half(tile_lo[:, n, :], i), half(raw_tile(g, n), i),
                                            half(tile_hi[:, n, :], i).bitcast(F32),
                                            ALU.subtract).then_inc(g.lo_ready, 1)

        @block.vector
        def _(dve):
            chain = Chain(dve, link)

            def m_low(t):
                dve.wait_ge(sem["m_hi"], t + 1)
                nc.vector.tensor_tensor(m_lo[:, t % 2, :, :], g.merged[:, :, t * P:(t + 1) * P],
                                        m_hi[:, t % 2, :, :].bitcast(F32), ALU.subtract).then_inc(sem["m_lo"], 1)

            m_low(0)
            for n in (2, 3):
                out_low(b, dve, g, n)
            m_low(1)
            dve.wait_ge(sem["rows_ready"], 2)
            for t in range(TT):
                x1t, h2t, st = x1[:, t % 2, :], h2[:, t % 2, :], stat[:, t % 2, :]
                dve.wait_ge(sem["mix_ps"], t + 1)
                if t >= 2:
                    dve.wait_ge(sem[f"stored_x1_{t % 2}"], 16 * (t // 2))
                dve.wait_ge(sem[f"x_in{t % 2}"], 16 * (t // 2 + 1))
                chain(nc.vector.tensor_tensor(x1t, mix(t), rows(0), ALU.mult))
                nc.vector.tensor_tensor(x1t, x1t, x[:, t % 2, :], ALU.add).then_inc(sem["x1_ready"], 1)
                if t + 2 < TT:
                    m_low(t + 2)
                dve.wait_ge(sem["rows_ready"], 6)
                dve.wait_ge(sem["std"], t + 1)
                chain(nc.vector.reciprocal(st[:, 2:3], st[:, 1:2]))
                chain(nc.vector.scalar_tensor_tensor(out=h2t, in0=x1t, scalar=st[:, 2:3], in1=rows(1),
                                                     op0=ALU.mult, op1=ALU.mult))
                nc.vector.tensor_tensor(h2t, h2t, rows(2), ALU.add).then_inc(sem["h2_ready"], 1)
                dve.wait_ge(sem["logit_ps"], t + 1)
                nc.vector.tensor_copy(logits[:, t % 4, t // 4, :], ps_log[:, 0:E]).then_inc(sem["logits"], 1)
            dve.wait_ge(sem["logits"], TT)
            chain(nc.vector.tensor_reduce(soft[:, 0, :], by_tile, AX.X, ALU.max))
            nc.vector.tensor_tensor(by_tile, by_tile, soft[:, 0, :].unsqueeze(2).to_broadcast([P, TT, E]),
                                    ALU.subtract).then_inc(sem["shifted"], 1)
            dve.wait_ge(sem["exped"], 1)
            chain(nc.vector.tensor_reduce(soft[:, 1, :], by_tile, AX.X, ALU.add))
            chain(nc.vector.reciprocal(soft[:, 2, :], soft[:, 1, :]))
            nc.vector.tensor_tensor(by_tile, by_tile, soft[:, 2, :].unsqueeze(2).to_broadcast([P, TT, E]),
                                    ALU.mult).then_inc(sem["affinity"], 1)
            dve.wait_ge(sem["aff_ready"], 1)
            for r in range(CAP // 8):
                eight = slice(8 * r, 8 * r + 8)
                chain(nc.vector.max(best[:, eight], aff))
                chain(nc.vector.max_index(best_at[:, eight], best[:, eight], aff))
                chain(nc.vector.match_replace(aff, best[:, eight], aff, -1.0))
            chain(nc.vector.tensor_copy(best_at_f, best_at[:, :]))
            chain(nc.vector.tensor_copy(best_up, best[:, ::-1]))
            nc.vector.tensor_copy(best_at_up, best_at_f[:, ::-1]).then_inc(sem["chosen"], 1)
            dve.wait_ge(sem["choice_ps"], 1)
            turned = ps_choice[:, 0:8 * E].rearrange("p (l h e) -> p l h e", h=2, e=E)
            early, early_at, late, late_at = turned[:, 0, 0, :], turned[:, 1, 0, :], turned[:, 2, 1, :], turned[:, 3, 1, :]
            chain(nc.vector.tensor_copy(pick[:, 0, :], early))
            chain(nc.vector.tensor_copy(pick[:, 1, :], early_at))
            chain(nc.vector.tensor_tensor(g.slot_gate[:, :], pick[:, 0, :], late, ALU.max))
            chain(nc.vector.tensor_tensor(pick[:, 0, :], pick[:, 0, :], late, ALU.is_ge))
            chain(nc.vector.scalar_tensor_tensor(out=pick[:, 1, :], in0=pick[:, 1, :], scalar=-float(T // 2), in1=late_at,
                                                 op0=ALU.add, op1=ALU.subtract))
            chain(nc.vector.tensor_tensor(pick[:, 1, :], pick[:, 1, :], pick[:, 0, :], ALU.mult))
            chain(nc.vector.scalar_tensor_tensor(out=g.slot_token[:, :], in0=pick[:, 1, :], scalar=float(T // 2),
                                                 in1=late_at, op0=ALU.add, op1=ALU.add))

        @block.tensor
        def _(pe):
            def row(r):
                for c in range(KC):
                    bank = row_banks(r)[c // 4]
                    last = nc.tensor.matmul(bank[:, c % 4 * P:(c % 4 + 1) * P],
                                            mod[:, row_cols[r] + c:row_cols[r] + c + 1].to_broadcast([P, P]), ident,
                                            start=True, stop=True)
                last.then_inc(sem["rows_ps"], 1)

            row(0)
            row(1)

            def router_of(t):
                pe.wait_ge(sem["h2_ready"], t + 1)
                if t:
                    pe.wait_ge(sem["tr_read"], t)
                for c in range(KC):
                    last = nc.tensor.transpose(flat_tr[:, c * P:(c + 1) * P], h2[:, t % 2, c * P:(c + 1) * P], ident)
                last.then_inc(sem["tr_ps"], 1)
                pe.wait_ge(sem["tr_read"], t + 1)
                if t:
                    pe.wait_ge(sem["logits"], t)
                for c in range(KC):
                    last = nc.tensor.matmul(ps_log[:, 0:E], h2_t[:, c, :], router[:, c, :],
                                            start=(c == 0), stop=(c == KC - 1))
                last.then_inc(sem["logit_ps"], 1)

            pe.wait_ge(sem["router_in"], 16)
            for t in range(TT):
                pe.wait_ge(sem["m_lo"], t + 1)
                if t >= 2:
                    pe.wait_ge(sem["x1_ready"], t - 1)
                for h in range(2):
                    for c in range(KC):
                        if t == 0 and h == 0 and c % 2 == 0:
                            pe.wait_ge(b.out_read, c // 2 + 1)
                        cols = slice(h * HALF, (h + 1) * HALF)
                        for m, (l, r) in enumerate(((m_hi, w_hi), (m_hi, w_lo), (m_lo, w_hi))):
                            last = nc.tensor.matmul(mix(t)[:, cols], l[:, t % 2, c, :], r[:, c, cols],
                                                    start=(c == 0 and m == 0), stop=(c == KC - 1 and m == 2))
                last.then_inc(sem["mix_ps"], 1)
                if t == 0:
                    pe.wait_ge(sem["rows_ready"], 2)
                    row(2)
                    pe.wait_ge(sem["rows_ready"], 6)
                else:
                    router_of(t - 1)
            router_of(TT - 1)
            pe.wait_ge(sem["affinity"], 1)
            pe.wait_ge(sem["tr_read"], TT)
            for t in range(4):
                last = nc.tensor.transpose(flat_tr[0:2 * E, t * P:(t + 1) * P],
                                           logits[:, t, :, :].rearrange("p b e -> p (b e)"), ident)
            last.then_inc(sem["aff_ps"], 1)
            pe.wait_ge(sem["chosen"], 1)
            for n in range(4):
                last = nc.tensor.transpose(ps_choice[:, 2 * E * n:2 * E * (n + 1)], lists[:, n, :],
                                           const[0:2 * E, C_ID:C_ID + 2 * E])
            last.then_inc(sem["choice_ps"], 1)


TILES = [("gate", 0), ("up", 0), ("gate", 1), ("up", 1), ("gate", 2), ("up", 2), ("down", 0),
         ("gate", 3), ("up", 3), ("down", 1), ("down", 2), ("down", 3)]
NT = len(TILES)
QUARTER = FF // 4
TILE = KC * QUARTER
RAW_TILES = 6
EARLY_TILES = 4
SPLIT_AHEAD = 2
FETCHED_AHEAD = RAW_TILES + SPLIT_AHEAD
TURNS = {2: 0, 4: 1, 7: 2, 8: "x", 9: 3}
TURN_ORDER = [0, 1, 2, "x", 3]


def split_rings(g):
    return (h[:, :, :].rearrange("p c n -> p (c n)").rearrange("p (s n) -> p s n", s=2) for h in (g.h_hi, g.h_lo))


def half(tile, i):
    return tile[:, i * TILE // 2:(i + 1) * TILE // 2]


def raw_tile(g, t):
    slot = t % RAW_TILES
    return g.tiles[:, slot, :] if slot < EARLY_TILES else g.late_tiles[:, slot - EARLY_TILES, :]


def fetch_tile(d, g, sp, e, t, lo_ready=None, split=None):
    kind, q = TILES[t]
    w = d["w_" + kind][0][e]
    if kind == "down":
        src = w.rearrange("(q c p) n -> q p c n", q=4, p=P)[q]
    else:
        src = w.rearrange("(c p) (q n) -> q p c n", p=P, q=4)[q]
    dst = raw_tile(g, t).rearrange("p (c n) -> p c n", n=D if kind == "down" else QUARTER)
    if split is not None:
        sp.wait_ge(lo_ready, 2 * split)
    sp.dma_start(dst, src).then_inc(g.tile_in[t % RAW_TILES], 16)


def stage_experts(b, g, out, h2_dram):
    nc, d = b.nc, b.dram
    with ExitStack() as ctx:
        tile_in = g.tile_in
        g.late_tiles = b.sb("late_tiles", [P, RAW_TILES - EARLY_TILES, TILE], ctx=ctx)
        w_hi, w_lo = split_rings(g)
        x = b.sb("moe_x", [P, D], ctx=ctx)
        x_hi, x_lo = b.sb("moe_x_hi", [P, KC, P], F32R, ctx), b.sb("moe_x_lo", [P, KC, P], F32R, ctx)
        hidden = b.sb("moe_hidden", [P, QUARTER], ctx=ctx)
        h_hi, h_lo = b.sb("moe_h_hi", [P, 4, 4, P], F32R, ctx), b.sb("moe_h_lo", [P, 4, 4, P], F32R, ctx)
        y, gate2 = b.sb("moe_y", [P, D], ctx=ctx), b.sb("moe_gate2", [P, D], ctx=ctx)
        gate_at = b.sb("gate_at", [P, 1], ctx=ctx)
        ps_gu, ps_down, ps_turn = b.ps("ps_gu", [P, 4, HALF], ctx), b.ps("ps_down", [P, 2, HALF], ctx), b.ps("ps_turn", [P, 2, HALF], ctx)
        hi_ready, lo_ready = g.hi_ready, g.lo_ready
        tile_done = b.sem("moe_tile_done")
        silu_ready, hidden_ready = b.sem("moe_silu_ready"), b.sem("moe_hidden_ready")
        turned, turn_hi, turn_lo = b.sem("moe_turned"), b.sem("moe_turn_hi"), b.sem("moe_turn_lo")
        gathered, scattered = b.sem("moe_gathered"), b.sem("moe_scattered")
        gate_set, y_free = b.sem("moe_gate_set"), b.sem("moe_y_free")
        y_ready, gate2_ps, gate2_ready = b.sem("moe_y_ready"), b.sem("moe_gate2_ps"), b.sem("moe_gate2_ready")
        block = ctx.enter_context(nc.Block())
        ident = g.const[:, C_ID:C_ID + P]
        flat_turn = ps_turn[:, :, :].rearrange("p a n -> p (a n)")
        flat_down = ps_down[:, :, :].rearrange("p a n -> p (a n)")
        gate_bank = lambda q: ps_gu[:, 2 * (q % 2), :]
        up_bank = lambda q: ps_gu[:, 2 * (q % 2) + 1, :]

        def turn_view(what):
            if what == "x":
                return flat_turn, x_hi[:, :, :].rearrange("p c n -> p (c n)"), x_lo[:, :, :].rearrange("p c n -> p (c n)")
            return (ps_turn[:, what % 2, :], h_hi[:, what, :, :].rearrange("p c n -> p (c n)"),
                    h_lo[:, what, :, :].rearrange("p c n -> p (c n)"))

        turns_before = lambda e, what: e * 5 + 1 + TURN_ORDER.index(what)

        @block.sync
        def _(sp):
            sp.wait_ge(gathered, 16)
            for t in range(EARLY_TILES, FETCHED_AHEAD):
                fetch_tile(d, g, sp, 0, t, lo_ready, t - RAW_TILES + 1 if t >= RAW_TILES else None)

            def expert(e, last=False):
                for t in range(FETCHED_AHEAD, NT if last else NT + FETCHED_AHEAD):
                    split = e * NT + t - RAW_TILES + 1
                    fetch_tile(d, g, sp, e if t < NT else e + 1, t % NT, lo_ready, split)

            with sp.Fori(0, E - 1) as e:
                expert(e)
            expert(E - 1, last=True)

        @block.scalar
        def _(act):
            def high(e, t):
                act.wait_ge(tile_in[t % RAW_TILES], e * (16 * NT // RAW_TILES) + 16 * (t // RAW_TILES + 1))
                if t >= 2:
                    act.wait_ge(tile_done, e * NT + t - 1)
                for i in range(2):
                    nc.scalar.activation(half(w_hi[:, t % 2, :], i), half(raw_tile(g, t), i), ACT.Copy).then_inc(hi_ready, 1)

            def turn(count, what):
                src, hi, _ = turn_view(what)
                act.wait_ge(turned, count)
                nc.scalar.activation(hi, src, ACT.Copy).then_inc(turn_hi, 1)

            act.wait_ge(gate2_ps, 1)
            nc.scalar.activation(gate2[:, :], flat_down, ACT.Copy).then_inc(gate2_ready, 1)
            turn(1, "x")

            def expert(e, last=False):
                for t, (kind, q) in enumerate(TILES):
                    if not last or t + SPLIT_AHEAD < NT:
                        high(e, t + SPLIT_AHEAD)
                    if t in TURNS and not (last and TURNS[t] == "x"):
                        count = turns_before(e, TURNS[t]) + 1
                        turn(count - 1 if last and t > 8 else count, TURNS[t])
                    if kind == "gate":
                        act.wait_ge(tile_done, e * NT + t + 1)
                        nc.scalar.activation(hidden[:, :], gate_bank(q), ACT.Silu).then_inc(silu_ready, 1)

            with act.Fori(0, E - 1) as e:
                expert(e)
            expert(E - 1, last=True)

        @block.vector
        def _(dve):
            def low(e, t):
                for i in range(2):
                    dve.wait_ge(hi_ready, e * (2 * NT) + 2 * t + i + 1)
                    nc.vector.tensor_tensor(half(w_lo[:, t % 2, :], i), half(raw_tile(g, t), i),
                                            half(w_hi[:, t % 2, :], i).bitcast(F32), ALU.subtract).then_inc(lo_ready, 1)

            def turn(count, what):
                src, hi, lo = turn_view(what)
                dve.wait_ge(turn_hi, count)
                nc.vector.tensor_tensor(lo, src, hi.bitcast(F32), ALU.subtract).then_inc(turn_lo, 1)

            turn(1, "x")

            def expert(e, last=False):
                for t, (kind, q) in enumerate(TILES):
                    if kind == "up":
                        dve.wait_ge(tile_done, e * NT + t + 1)
                        dve.wait_ge(silu_ready, e * 4 + q + 1)
                        nc.vector.tensor_tensor(hidden[:, :], hidden[:, :], up_bank(q), ALU.mult).then_inc(hidden_ready, 1)
                    if not last or t + SPLIT_AHEAD < NT:
                        low(e, t + SPLIT_AHEAD)
                    if t in TURNS and not (last and TURNS[t] == "x"):
                        count = turns_before(e, TURNS[t]) + 1
                        turn(count - 1 if last and t > 8 else count, TURNS[t])
                dve.wait_ge(tile_done, e * NT + NT)
                dve.wait_ge(gate_set, e + 1)
                dve.wait_ge(y_free, e + 1)
                for i in range(2):
                    cols = slice(i * HALF, (i + 1) * HALF)
                    nc.vector.scalar_tensor_tensor(out=y[:, cols], in0=ps_down[:, i, :], scalar=gate_at[:, 0:1],
                                                   in1=gate2[:, cols], op0=ALU.mult, op1=ALU.mult
                                                   ).then_inc(y_ready, 1)

            dve.wait_ge(gate2_ready, 1)
            with dve.Fori(0, E - 1) as e:
                expert(e)
            expert(E - 1, last=True)

        @block.gpsimd
        def _(pool):
            def gather(e):
                nc.gpsimd.indirect_dma_start(x[:, :], None, h2_dram,
                                             bass.IndirectOffsetOnAxis(g.slot_token[:, e:e + 1], 0)
                                             ).then_inc(gathered, 16)

            gather(0)
            for e in range(E):
                nc.gpsimd.tensor_copy(gate_at[:, :], g.slot_gate[:, e:e + 1]).then_inc(gate_set, 1)
                if e + 1 < E:
                    pool.wait_ge(turned, 5 * e + 1)
                    gather(e + 1)
                if e:
                    pool.wait_ge(scattered, 16 * e)
                pool.sem_inc(y_free, 1)
                pool.wait_ge(y_ready, 2 * e + 2)
                nc.gpsimd.indirect_dma_start(out[0], bass.IndirectOffsetOnAxis(g.slot_token[:, e:e + 1], 0),
                                             y[:, :], None, compute_op=ALU.add).then_inc(scattered, 16)
            pool.wait_ge(scattered, 16 * E)

        @block.tensor
        def _(pe):
            for c in range(KC):
                last_mm = nc.tensor.matmul(flat_down[:, c * P:(c + 1) * P], g.mod[:, 40 + c:41 + c].to_broadcast([P, P]), ident,
                                           start=True, stop=True)
            last_mm.then_inc(gate2_ps, 1)

            def turn(what):
                src, n = (x, KC) if what == "x" else (hidden, 4)
                dst = turn_view(what)[0]
                for c in range(n):
                    ins = nc.tensor.transpose(dst[:, c * P:(c + 1) * P], src[:, c * P:(c + 1) * P], ident)
                ins.then_inc(turned, 1)

            def product(bank, lhs_hi, lhs_lo, t, c, cols, start, stop):
                for m, (a, w) in enumerate(((lhs_hi, w_hi), (lhs_hi, w_lo), (lhs_lo, w_hi))):
                    ins = nc.tensor.matmul(bank, a, w[:, t % 2, cols], start=start and m == 0, stop=stop and m == 2)
                return ins

            pe.wait_ge(gathered, 16)
            turn("x")
            pe.wait_ge(gate2_ready, 1)

            def expert(e, last=False):
                pe.wait_ge(turn_lo, e * 5 + 1)
                for t, (kind, q) in enumerate(TILES):
                    if kind == "down":
                        pe.wait_ge(turn_lo, (e * 5 + 5) if last and q == 3 else turns_before(e, q) + 1)
                        if q == 0:
                            pe.wait_ge(gate_set, e + 1)
                    for i in range(2):
                        pe.wait_ge(lo_ready, e * (2 * NT) + 2 * t + i + 1)
                        if kind == "down":
                            for c in range(2 * i, 2 * i + 2):
                                for n in range(2):
                                    ins = product(ps_down[:, n, :], h_hi[:, q, c, :], h_lo[:, q, c, :], t, c,
                                                  slice(c * D + n * HALF, c * D + (n + 1) * HALF),
                                                  q == 0 and c == 0, q == 3 and c == 3)
                        else:
                            bank = gate_bank(q) if kind == "gate" else up_bank(q)
                            for c in range(4 * i, 4 * i + 4):
                                ins = product(bank, x_hi[:, c, :], x_lo[:, c, :], t, c,
                                              slice(c * QUARTER, (c + 1) * QUARTER), c == 0, c == KC - 1)
                    ins.then_inc(tile_done, 1)
                    if t in TURNS:
                        what = TURNS[t]
                        if what == "x":
                            if last:
                                continue
                            pe.wait_ge(gathered, e * 16 + 32)
                            pe.wait_ge(turn_lo, turns_before(e, "x"))
                        else:
                            pe.wait_ge(hidden_ready, e * 4 + what + 1)
                            if what == 3:
                                pe.wait_ge(turn_lo, (e * 5 + 4) if last else turns_before(e, 3))
                        turn(what)

            with pe.Fori(0, E - 1) as e:
                expert(e)
            expert(E - 1, last=True)


class Shared:
    pass


INPUTS = ["x", "c", "positions", "w_ada", "b_ada", "norm1_w", "w_in", "q_norm_w", "k_norm_w", "conv_w",
          "conv_b", "lru_w_a", "lru_b_a", "lru_w_x", "lru_b_x", "lru_lambda", "w_attn_branch",
          "w_lru_branch", "w_out", "norm2_w", "w_router", "w_gate", "w_up", "w_down", "const"]


def program(nc, dram, out):
    with ExitStack() as ctx:
        b = Build(nc, ctx, dram)
        g = Shared()
        g.const = b.sb("const", [P, C_END])
        g.par_a, g.par_b = b.sb("par_a", [P, A_END]), b.sb("par_b", [P, B_END])
        g.mod, g.cact, g.acc = b.sb("mod", [P, 48]), b.sb("silu_c", [P, KC]), b.sb("acc", [P, 2, UNIT])
        g.acc_free = b.sem("acc_free")
        g.slot_gate, g.slot_token = b.sb("slot_gate", [P, E]), b.sb("slot_token", [P, E], U32)
        g.tiles = b.sb("tiles", [P, EARLY_TILES, TILE])
        g.tile_in = [b.sem(f"moe_tile_in{s}") for s in range(RAW_TILES)]
        flat_tiles = g.tiles[:, :, :].rearrange("p s n -> p (s n)")
        ring_end = RAW * KC * UNIT
        g.area = flat_tiles[:, ring_end:]
        g.h_hi, g.h_lo = b.sb("h_hi", [P, KC, T], F32R), b.sb("h_lo", [P, KC, T], F32R)
        g.hi_ready, g.lo_ready = b.sem("moe_hi_ready"), b.sem("moe_lo_ready")
        with ExitStack() as mixer:
            b.rings(mixer, flat_tiles[:, 0:ring_end])
            g.attn_t = b.sb("attn_t", [P, 2, T], ctx=mixer)
            stage_norm(b, g)
            with ExitStack() as qkv:
                in_area = (EARLY_TILES * TILE - ring_end) // T
                k_rest = b.sb("k_rest", [P, 2 * QK_CHUNKS - in_area, T], ctx=qkv)
                g.qk = lambda n: g.area[:, n * T:(n + 1) * T] if n < in_area else k_rest[:, n - in_area, :]
                g.v = b.sb("v", [P, GROUPS, TT, UNIT], ctx=qkv)
                stage_qkv(b, g)
                stage_attention(b, g)
            g.lru_t = b.sb("lru_t", [P, KC, T], ctx=mixer)
            with ExitStack() as banks:
                g.ps_proj = b.ps("ps_projected", [P, 4, HALF], banks)
                stage_lru(b, g)
                g.merged = g.area[:, 0:KC * T].rearrange("p (c n) -> p c n", n=T)
                stage_merge(b, g)
            h2_dram = nc.dram_tensor("h2_rows", (T, D), F32).ap()
            stage_out(b, g, out, h2_dram)
        stage_experts(b, g, out, h2_dram)


def kernel(**inputs):
    import concourse.bacc as bacc
    from concourse.bass_utils import run_bass_kernel_spmd

    nc = bacc.Bacc("TRN2", target_bir_lowering=False, num_devices=1)
    arrays, dram = {}, {}
    for name in INPUTS:
        a = constants() if name == "const" else np.ascontiguousarray(inputs[name])
        arrays[f"in_{name}"] = a
        dram[name] = nc.dram_tensor(f"in_{name}", a.shape, mybir.dt.from_np(a.dtype), kind="ExternalInput").ap()
    out = nc.dram_tensor("out_x", (1, T, D), F32, kind="ExternalOutput").ap()
    program(nc, dram, out)
    r = run_bass_kernel_spmd(nc, [arrays], core_ids=[0])
    return r.results[0]["out_x"]
```
